# Optimizing a Trainium2 kernel written in Bass

```python
import jax, jax.numpy as jnp
from jax import lax
import numpy as np

D_MODEL = 1024
BATCH = 1
SEQ = 512
DEPTH = 2

N_META = 16
BLOCK = 128
WINDOW = 128
RET_HEADS = 8
RET_QK_DIM = D_MODEL // 16
RET_V_DIM = D_MODEL // 8
ATT_Q_HEADS = 8
ATT_KV_HEADS = 2
ATT_GROUP = ATT_Q_HEADS // ATT_KV_HEADS
ATT_HEAD_DIM = D_MODEL // 16
ROPE_DIM = ATT_HEAD_DIM // 4
ROPE_THETA = 500000.0
XPOS_THETA = 10000.0
D_FF = 4 * D_MODEL
EPS = 1e-6
NEG_INF = -1e30

RET_QK = RET_HEADS * RET_QK_DIM
RET_V = RET_HEADS * RET_V_DIM
ATT_Q = ATT_Q_HEADS * ATT_HEAD_DIM
ATT_KV = ATT_KV_HEADS * ATT_HEAD_DIM
SPLITS = (RET_QK, RET_QK, RET_V, RET_V, ATT_Q, ATT_KV, ATT_KV, D_MODEL, D_MODEL)
D_IN = sum(SPLITS)


def rms_norm(x, g):
    xf = x.astype(jnp.float32)
    y = xf * lax.rsqrt(jnp.mean(xf * xf, axis=-1, keepdims=True) + EPS)
    return (y * g.astype(jnp.float32)).astype(x.dtype)

def rotate(x, pos, theta, rot_dim):
    half = rot_dim // 2
    freqs = jnp.power(jnp.float32(theta), -jnp.arange(0, rot_dim, 2, dtype=jnp.float32) / rot_dim)
    ang = pos.astype(jnp.float32)[:, None] * freqs[None, :]
    cos = jnp.cos(ang)[:, None, :]
    sin = jnp.sin(ang)[:, None, :]
    xf = x.astype(jnp.float32)
    x1, x2 = xf[..., :half], xf[..., half:rot_dim]
    out = jnp.concatenate([x1 * cos - x2 * sin, x2 * cos + x1 * sin, xf[..., rot_dim:]], axis=-1)
    return out.astype(x.dtype)

def retention_dir(q, k, v, log_gamma, include_diag):
    C = q.shape[-2]
    idx = jnp.arange(C, dtype=jnp.float32)
    rel = idx[:, None] - idx[None, :]
    lg = log_gamma[:, None, None]
    mask = (rel >= 0) if include_diag else (rel > 0)
    decay_in = jnp.where(mask[None], jnp.exp(lg * jnp.maximum(rel, 0.0)[None]), 0.0)
    s = jnp.einsum('bhncd,bhnkd->bhnck', q, k) * decay_in[:, None]
    o_in = jnp.einsum('bhnck,bhnke->bhnce', s, v)
    k_dec = k * jnp.exp(lg * (C - 1 - idx)[None, :])[:, None, :, :].transpose(0, 1, 3, 2)
    kv = jnp.einsum('bhncd,bhnce->bhnde', k_dec, v)
    chunk_decay = jnp.exp(log_gamma * C)[:, None, None]

    def step(state, kv_n):
        return state * chunk_decay + kv_n, state

    init = jnp.zeros(kv.shape[:2] + kv.shape[3:], jnp.float32)
    _, s_prev = lax.scan(step, init, jnp.moveaxis(kv, 2, 0))
    s_prev = jnp.moveaxis(s_prev, 0, 2)
    q_dec = q * jnp.exp(lg * (idx + 1.0)[None, :])[:, None, :, :].transpose(0, 1, 3, 2)
    o_x = jnp.einsum('bhncd,bhnde->bhnce', q_dec, s_prev)
    return o_in + o_x

def retention_branch(q, k, v, gate, log_decay, pad):
    B, L = q.shape[:2]
    Lp = L + pad
    nc = Lp // BLOCK
    pos = jnp.arange(L)
    q = rotate(q, pos, XPOS_THETA, RET_QK_DIM) * (RET_QK_DIM ** -0.5)
    k = rotate(k, pos, XPOS_THETA, RET_QK_DIM)

    def chunk(t):
        t = jnp.pad(t.astype(jnp.float32), ((0, 0), (pad, 0), (0, 0), (0, 0)))
        return t.reshape(B, nc, BLOCK, t.shape[2], t.shape[3]).transpose(0, 3, 1, 2, 4)

    qc, kc, vc = chunk(q), chunk(k), chunk(v)
    flip = lambda t: t[:, :, ::-1, ::-1]
    o = retention_dir(qc, kc, vc, log_decay[0], True) + flip(
        retention_dir(flip(qc), flip(kc), flip(vc), log_decay[1], False))
    o = o.transpose(0, 2, 3, 1, 4).reshape(B, Lp, RET_HEADS, RET_V_DIM)[:, pad:]
    mu = jnp.mean(o, axis=-1, keepdims=True)
    var = jnp.mean(jnp.square(o - mu), axis=-1, keepdims=True)
    o = (o - mu) * lax.rsqrt(var + EPS)
    o = o.reshape(B, L, RET_V).astype(gate.dtype)
    return o * jax.nn.silu(gate)

def attention_branch(q, k, v, sink, pad):
    B, L = q.shape[:2]
    Lp = L + pad
    nb = Lp // BLOCK
    pos = jnp.arange(L)
    q = rotate(q, pos, ROPE_THETA, ROPE_DIM)
    k = rotate(k, pos, ROPE_THETA, ROPE_DIM)
    meta_k, meta_v = k[:, :N_META], v[:, :N_META]
    qb = jnp.pad(q, ((0, 0), (pad, 0), (0, 0), (0, 0))).reshape(
        B, nb, BLOCK, ATT_KV_HEADS, ATT_GROUP, ATT_HEAD_DIM)
    ext = ((0, 0), (pad + BLOCK, BLOCK), (0, 0), (0, 0))
    kb = jnp.pad(k, ext).reshape(B, nb + 2, BLOCK, ATT_KV_HEADS, ATT_HEAD_DIM)
    vb = jnp.pad(v, ext).reshape(B, nb + 2, BLOCK, ATT_KV_HEADS, ATT_HEAD_DIM)

    def band(t):
        return jnp.concatenate([t[:, :-2], t[:, 1:-1], t[:, 2:]], axis=2)

    kband, vband = band(kb), band(vb)
    qpos = jnp.arange(nb)[:, None] * BLOCK + jnp.arange(BLOCK)[None, :]
    kpos = (jnp.arange(nb)[:, None] - 1) * BLOCK + jnp.arange(3 * BLOCK)[None, :]
    valid = ((kpos[:, None, :] >= pad + N_META) & (kpos[:, None, :] < Lp)
             & (jnp.abs(qpos[:, :, None] - kpos[:, None, :]) <= WINDOW))
    scale = ATT_HEAD_DIM ** -0.5
    s_band = jnp.einsum('bnqgrd,bnkgd->bngrqk', qb, kband).astype(jnp.float32) * scale
    s_band = jnp.where(valid[None, :, None, None], s_band, NEG_INF)
    s_meta = jnp.einsum('bnqgrd,bmgd->bngrqm', qb, meta_k).astype(jnp.float32) * scale
    s_sink = jnp.broadcast_to(sink.astype(jnp.float32).reshape(1, 1, ATT_KV_HEADS, ATT_GROUP, 1, 1),
                              s_meta.shape[:-1] + (1,))
    p = jax.nn.softmax(jnp.concatenate([s_sink, s_meta, s_band], axis=-1), axis=-1).astype(v.dtype)
    o = (jnp.einsum('bngrqm,bmgd->bnqgrd', p[..., 1:1 + N_META], meta_v)
         + jnp.einsum('bngrqk,bnkgd->bnqgrd', p[..., 1 + N_META:], vband))
    return o.reshape(B, Lp, ATT_Q)[:, pad:]

def first_inputs(seed: int = 0) -> dict:
    key = jax.random.key(seed)
    ks = jax.random.split(key, 14)
    f = jnp.float32
    nrm = lambda k, shape, s: jax.random.normal(k, shape, f) * s
    heads = np.arange(RET_HEADS)
    base = np.log(-np.log(1.0 - 2.0 ** (-5.0 - heads))).astype(np.float32)
    return {
        "x": nrm(ks[0], (BATCH, SEQ, D_MODEL), 1.0),
        "meta_tokens": nrm(ks[1], (N_META, D_MODEL), 1.0),
        "w_in": nrm(ks[2], (DEPTH, D_MODEL, D_IN), D_MODEL ** -0.5),
        "w_ret_o": nrm(ks[3], (DEPTH, RET_V, D_MODEL), RET_V ** -0.5),
        "w_att_o": nrm(ks[4], (DEPTH, ATT_Q, D_MODEL), ATT_Q ** -0.5),
        "w_mix_o": nrm(ks[5], (DEPTH, D_MODEL, D_MODEL), D_MODEL ** -0.5),
        "w_ff1": nrm(ks[6], (DEPTH, D_MODEL, D_FF), D_MODEL ** -0.5),
        "w_ff2": nrm(ks[7], (DEPTH, D_FF, D_MODEL), D_FF ** -0.5),
        "norm_mix_pre": 1.0 + nrm(ks[8], (DEPTH, D_MODEL), 0.02),
        "norm_mix_post": 1.0 + nrm(ks[9], (DEPTH, D_MODEL), 0.02),
        "norm_ff_pre": 1.0 + nrm(ks[10], (DEPTH, D_MODEL), 0.02),
        "norm_ff_post": 1.0 + nrm(ks[11], (DEPTH, D_MODEL), 0.02),
        "ret_decay": jnp.asarray(base)[None, None, :] + nrm(ks[12], (DEPTH, 2, RET_HEADS), 0.05),
        "attn_sink": nrm(ks[13], (DEPTH, ATT_Q_HEADS), 0.5),
    }

def first_block(x, meta_tokens, w_in, w_ret_o, w_att_o, w_mix_o, w_ff1, w_ff2,
              norm_mix_pre, norm_mix_post, norm_ff_pre, norm_ff_post, ret_decay, attn_sink):
    B = x.shape[0]
    h = jnp.concatenate([jnp.broadcast_to(meta_tokens[None].astype(x.dtype), (B, N_META, D_MODEL)), x], axis=1)
    L = h.shape[1]
    pad = (-L) % BLOCK
    for l in range(DEPTH):
        u = rms_norm(h, norm_mix_pre[l])
        proj = u @ w_in[l]
        parts, off = [], 0
        for size in SPLITS:
            parts.append(proj[..., off:off + size])
            off += size
        q_r, k_r, v_r, g_r, q_a, k_a, v_a, gate_r, gate_a = parts
        log_decay = -jnp.exp(ret_decay[l].astype(jnp.float32))
        y_r = retention_branch(q_r.reshape(B, L, RET_HEADS, RET_QK_DIM),
                               k_r.reshape(B, L, RET_HEADS, RET_QK_DIM),
                               v_r.reshape(B, L, RET_HEADS, RET_V_DIM),
                               g_r, log_decay, pad) @ w_ret_o[l]
        y_a = attention_branch(q_a.reshape(B, L, ATT_Q_HEADS, ATT_HEAD_DIM),
                               k_a.reshape(B, L, ATT_KV_HEADS, ATT_HEAD_DIM),
                               v_a.reshape(B, L, ATT_KV_HEADS, ATT_HEAD_DIM),
                               attn_sink[l], pad) @ w_att_o[l]
        mix = (jax.nn.sigmoid(gate_r) * y_r + jax.nn.sigmoid(gate_a) * y_a) @ w_mix_o[l]
        h = h + rms_norm(mix, norm_mix_post[l])
        u = rms_norm(h, norm_ff_pre[l])
        ff = jnp.square(jax.nn.relu(u @ w_ff1[l])) @ w_ff2[l]
        h = h + rms_norm(ff, norm_ff_post[l])
    return h[:, N_META:]


DEPTH_2 = 1

CHUNK = 64
MEM_LEN = 256
CONV_W = 4

GDN_HEADS = 4
GDN_DK = 128
GDN_DV = 128
GDN_QK = GDN_HEADS * GDN_DK
GDN_VD = GDN_HEADS * GDN_DV
LRU_DIM = D_MODEL // 2
LRU_BLOCKS = 8
LRU_BW = LRU_DIM // LRU_BLOCKS
LRU_C = 8.0
MIX_DIM = GDN_VD + LRU_DIM
IN_SPLITS = (3 * GDN_QK, GDN_VD, GDN_HEADS, GDN_HEADS, LRU_DIM, LRU_DIM)
IN_COLS = 3 * GDN_QK + GDN_VD + 2 * GDN_HEADS + 2 * LRU_DIM

XA_HEADS = 4
XA_DH = D_MODEL // XA_HEADS

PEER_HEADS = 8
PEER_NKEYS = 128
PEER_N = PEER_NKEYS * PEER_NKEYS
PEER_DQ = 256
PEER_DH = PEER_DQ // 2
PEER_TOPK = 16
PEER_BLOCK = 128


def rmsnorm(x, w):
    xf = x.astype(jnp.float32)
    y = xf * lax.rsqrt(jnp.mean(xf * xf, axis=-1, keepdims=True) + EPS)
    return (y * w.astype(jnp.float32)).astype(x.dtype)

def l2norm(x):
    return x * lax.rsqrt(jnp.sum(x * x, axis=-1, keepdims=True) + EPS)

def causal_dwconv(x, w, b=None):
    s = x.shape[1]
    xp = jnp.pad(x, ((0, 0), (CONV_W - 1, 0), (0, 0)))
    y = sum(xp[:, j:j + s] * w[j] for j in range(CONV_W))
    return y if b is None else y + b

def gated_delta_rule(q, k, v, g, beta):
    bsz, s, h, dk = q.shape
    dv = v.shape[-1]
    n = s // CHUNK
    f32 = jnp.float32
    q = l2norm(q.astype(f32)) * (dk ** -0.5)
    k = l2norm(k.astype(f32))
    v = v.astype(f32)

    def chunks(t):
        return t.reshape(bsz, n, CHUNK, h, -1).transpose(0, 3, 1, 2, 4)

    qc, kc, vc = chunks(q), chunks(k), chunks(v)
    gc = g.astype(f32).reshape(bsz, n, CHUNK, h).transpose(0, 3, 1, 2)
    bc = beta.astype(f32).reshape(bsz, n, CHUNK, h).transpose(0, 3, 1, 2)
    gcum = jnp.cumsum(gc, axis=-1)
    pos = jnp.arange(CHUNK)
    causal = pos[:, None] >= pos[None, :]
    strict = pos[:, None] > pos[None, :]
    decay = jnp.exp(jnp.where(causal, gcum[..., :, None] - gcum[..., None, :], -jnp.inf))
    kb = kc * bc[..., None]
    vb = vc * bc[..., None]
    a_mat = jnp.where(strict, jnp.einsum('bhncd,bhnsd->bhncs', kb, kc) * decay, 0.0)
    t_mat = a_mat + jnp.eye(CHUNK, dtype=f32)
    rhs = jnp.concatenate([vb, kb * jnp.exp(gcum)[..., None]], axis=-1)
    sol = lax.linalg.triangular_solve(t_mat, rhs, left_side=True, lower=True, unit_diagonal=True)
    u, w = sol[..., :dv], sol[..., dv:]
    attn = jnp.where(causal, jnp.einsum('bhncd,bhnsd->bhncs', qc, kc) * decay, 0.0)
    q_dec = qc * jnp.exp(gcum)[..., None]
    k_dec = kc * jnp.exp(gcum[..., -1:] - gcum)[..., None]
    chunk_decay = jnp.exp(gcum[..., -1])

    def step(state, xs):
        q_i, w_i, u_i, a_i, k_i, d_i = xs
        v_new = u_i - jnp.einsum('bhcd,bhdv->bhcv', w_i, state)
        o = jnp.einsum('bhcd,bhdv->bhcv', q_i, state) + jnp.einsum('bhcs,bhsv->bhcv', a_i, v_new)
        state = state * d_i[..., None, None] + jnp.einsum('bhcd,bhcv->bhdv', k_i, v_new)
        return state, o

    xs = tuple(jnp.moveaxis(t, 2, 0) for t in (q_dec, w, u, attn, k_dec, chunk_decay))
    state0 = jnp.zeros((bsz, h, dk, dv), f32)
    _, o = lax.scan(step, state0, xs)
    return o.transpose(1, 0, 3, 2, 4).reshape(bsz, s, h, dv)

def rg_lru(xr, w_a, b_a, w_x, b_x, lam):
    bsz, s, c = xr.shape
    f32 = jnp.float32
    xf = xr.astype(f32)
    xb = xf.reshape(bsz, s, LRU_BLOCKS, LRU_BW)
    r = jax.nn.sigmoid(jnp.einsum('bsgi,gij->bsgj', xb, w_a.astype(f32)).reshape(bsz, s, c) + b_a.astype(f32))
    i = jax.nn.sigmoid(jnp.einsum('bsgi,gij->bsgj', xb, w_x.astype(f32)).reshape(bsz, s, c) + b_x.astype(f32))
    log_a = -LRU_C * r * jax.nn.softplus(-lam.astype(f32))
    a = jnp.exp(log_a)
    b_term = jnp.sqrt(-jnp.expm1(2.0 * log_a)) * (i * xf)

    def combine(c1, c2):
        a1, b1 = c1
        a2, b2 = c2
        return a1 * a2, a2 * b1 + b2

    _, hs = lax.associative_scan(combine, (a, b_term), axis=1)
    return hs

def hybrid_mixer(h, w_in, conv_qkv_w, gdn_a_log, gdn_dt_bias, gdn_norm_w,
                 lru_conv_w, lru_conv_b, lru_wa, lru_ba, lru_wx, lru_bx, lru_lambda, w_out):
    bsz, s, _ = h.shape
    f32 = jnp.float32
    proj = h @ w_in
    offs = np.cumsum(IN_SPLITS)[:-1].tolist()
    qkv, z, a_in, b_in, xr, gate = jnp.split(proj, offs, axis=-1)
    qkv = jax.nn.silu(causal_dwconv(qkv, conv_qkv_w))
    q, k, v = jnp.split(qkv, [GDN_QK, 2 * GDN_QK], axis=-1)
    g = -jnp.exp(gdn_a_log.astype(f32)) * jax.nn.softplus(a_in.astype(f32) + gdn_dt_bias.astype(f32))
    beta = jax.nn.sigmoid(b_in.astype(f32))
    o = gated_delta_rule(q.reshape(bsz, s, GDN_HEADS, GDN_DK), k.reshape(bsz, s, GDN_HEADS, GDN_DK),
                         v.reshape(bsz, s, GDN_HEADS, GDN_DV), g, beta)
    o = rmsnorm(o, gdn_norm_w) * jax.nn.silu(z.reshape(bsz, s, GDN_HEADS, GDN_DV).astype(f32))
    y_gdn = o.reshape(bsz, s, GDN_VD).astype(h.dtype)
    xr = causal_dwconv(xr, lru_conv_w, lru_conv_b)
    y_lru = (rg_lru(xr, lru_wa, lru_ba, lru_wx, lru_bx, lru_lambda) * jax.nn.gelu(gate.astype(f32))).astype(h.dtype)
    return jnp.concatenate([y_gdn, y_lru], axis=-1) @ w_out

def memory_cross_attention(h, mem_n, wq, wkv, wo):
    bsz, s, _ = h.shape
    m = mem_n.shape[1]
    f32 = jnp.float32
    q = (h @ wq).reshape(bsz, s, XA_HEADS, XA_DH)
    kv = (mem_n @ wkv).reshape(bsz, m, 2, XA_HEADS, XA_DH)
    k, v = kv[:, :, 0], kv[:, :, 1]
    scores = jnp.einsum('bshd,bmhd->bhsm', q.astype(f32), k.astype(f32)) * (XA_DH ** -0.5)
    p = jax.nn.softmax(scores, axis=-1)
    o = jnp.einsum('bhsm,bmhd->bshd', p, v.astype(f32)).reshape(bsz, s, XA_HEADS * XA_DH).astype(h.dtype)
    return o @ wo

def peer_ffn(h, wq, subkeys, u_tab, v_tab):
    bsz, s, d = h.shape
    t = h.reshape(bsz * s, d)
    ntok = t.shape[0]
    f32 = jnp.float32
    q = (t @ wq).reshape(ntok, PEER_HEADS, 2, PEER_DH).astype(f32)
    sc = jnp.einsum('thpd,hpkd->thpk', q, subkeys.astype(f32))
    s1, i1 = lax.top_k(sc[:, :, 0], PEER_TOPK)
    s2, i2 = lax.top_k(sc[:, :, 1], PEER_TOPK)
    cand = (s1[..., :, None] + s2[..., None, :]).reshape(ntok, PEER_HEADS, PEER_TOPK * PEER_TOPK)
    best, pos = lax.top_k(cand, PEER_TOPK)
    e1 = jnp.take_along_axis(i1, pos // PEER_TOPK, axis=-1)
    e2 = jnp.take_along_axis(i2, pos % PEER_TOPK, axis=-1)
    idx = e1 * PEER_NKEYS + e2
    gate = jax.nn.softmax(best, axis=-1).astype(h.dtype)
    nb = ntok // PEER_BLOCK

    def block(args):
        tb, ib, gb = args
        act = jax.nn.gelu(jnp.einsum('phkd,pd->phk', u_tab[ib], tb)) * gb
        return jnp.einsum('phk,phkd->pd', act, v_tab[ib])

    out = lax.map(block, (t.reshape(nb, PEER_BLOCK, d),
                          idx.reshape(nb, PEER_BLOCK, PEER_HEADS, PEER_TOPK),
                          gate.reshape(nb, PEER_BLOCK, PEER_HEADS, PEER_TOPK)))
    return out.reshape(bsz, s, d)

def second_inputs(seed: int = 0) -> dict:
    key = jax.random.key(seed)
    ks = jax.random.split(key, 32)
    f32 = jnp.float32
    L = DEPTH_2

    def nrm(k, shape, scale):
        return jax.random.normal(k, shape, f32) * scale

    def gain(k, shape):
        return 1.0 + 0.05 * jax.random.normal(k, shape, f32)

    x = nrm(ks[0], (BATCH, SEQ, D_MODEL), 1.0)
    mem = nrm(ks[1], (BATCH, MEM_LEN, D_MODEL), 1.0)
    norm_mix_w = gain(ks[2], (L, D_MODEL))
    w_in = nrm(ks[3], (L, D_MODEL, IN_COLS), D_MODEL ** -0.5)
    conv_qkv_w = nrm(ks[4], (L, CONV_W, 3 * GDN_QK), 0.5)
    gdn_a_log = jnp.log(jax.random.uniform(ks[5], (L, GDN_HEADS), f32, 1.0, 16.0))
    dt = jnp.exp(jax.random.uniform(ks[6], (L, GDN_HEADS), f32, np.log(1e-3), np.log(1e-1)))
    gdn_dt_bias = dt + jnp.log(-jnp.expm1(-dt))
    gdn_norm_w = gain(ks[7], (L, GDN_DV))
    lru_conv_w = nrm(ks[8], (L, CONV_W, LRU_DIM), 0.5)
    lru_conv_b = nrm(ks[9], (L, LRU_DIM), 0.01)
    lru_wa = nrm(ks[10], (L, LRU_BLOCKS, LRU_BW, LRU_BW), LRU_BW ** -0.5)
    lru_ba = nrm(ks[11], (L, LRU_DIM), 0.01)
    lru_wx = nrm(ks[12], (L, LRU_BLOCKS, LRU_BW, LRU_BW), LRU_BW ** -0.5)
    lru_bx = nrm(ks[13], (L, LRU_DIM), 0.01)
    a0 = jax.random.uniform(ks[14], (L, LRU_DIM), f32, 0.9, 0.999)
    a_base = a0 ** (1.0 / LRU_C)
    lru_lambda = jnp.log(a_base) - jnp.log1p(-a_base)
    w_out = nrm(ks[15], (L, MIX_DIM, D_MODEL), MIX_DIM ** -0.5)
    norm_xattn_w = gain(ks[16], (L, D_MODEL))
    norm_mem_w = gain(ks[17], (L, D_MODEL))
    xattn_wq = nrm(ks[18], (L, D_MODEL, XA_HEADS * XA_DH), D_MODEL ** -0.5)
    xattn_wkv = nrm(ks[19], (L, D_MODEL, 2 * XA_HEADS * XA_DH), D_MODEL ** -0.5)
    xattn_wo = nrm(ks[20], (L, XA_HEADS * XA_DH, D_MODEL), (XA_HEADS * XA_DH) ** -0.5)
    norm_ffn_w = gain(ks[21], (L, D_MODEL))
    peer_wq = nrm(ks[22], (L, D_MODEL, PEER_HEADS * PEER_DQ), D_MODEL ** -0.5)
    peer_subkeys = nrm(ks[23], (L, PEER_HEADS, 2, PEER_NKEYS, PEER_DH), PEER_DH ** -0.5)
    peer_u = nrm(ks[24], (L, PEER_N, D_MODEL), D_MODEL ** -0.5)
    peer_v = nrm(ks[25], (L, PEER_N, D_MODEL), PEER_HEADS ** -0.5)
    norm_final_w = gain(ks[26], (D_MODEL,))
    return {'x': x, 'mem': mem, 'norm_mix_w': norm_mix_w, 'w_in': w_in, 'conv_qkv_w': conv_qkv_w,
            'gdn_a_log': gdn_a_log, 'gdn_dt_bias': gdn_dt_bias, 'gdn_norm_w': gdn_norm_w,
            'lru_conv_w': lru_conv_w, 'lru_conv_b': lru_conv_b, 'lru_wa': lru_wa, 'lru_ba': lru_ba,
            'lru_wx': lru_wx, 'lru_bx': lru_bx, 'lru_lambda': lru_lambda, 'w_out': w_out,
            'norm_xattn_w': norm_xattn_w, 'norm_mem_w': norm_mem_w, 'xattn_wq': xattn_wq,
            'xattn_wkv': xattn_wkv, 'xattn_wo': xattn_wo, 'norm_ffn_w': norm_ffn_w,
            'peer_wq': peer_wq, 'peer_subkeys': peer_subkeys, 'peer_u': peer_u, 'peer_v': peer_v,
            'norm_final_w': norm_final_w}

def second_block(x, mem, norm_mix_w, w_in, conv_qkv_w, gdn_a_log, gdn_dt_bias, gdn_norm_w,
              lru_conv_w, lru_conv_b, lru_wa, lru_ba, lru_wx, lru_bx, lru_lambda, w_out,
              norm_xattn_w, norm_mem_w, xattn_wq, xattn_wkv, xattn_wo, norm_ffn_w,
              peer_wq, peer_subkeys, peer_u, peer_v, norm_final_w):
    for l in range(DEPTH_2):
        x = x + hybrid_mixer(rmsnorm(x, norm_mix_w[l]), w_in[l], conv_qkv_w[l], gdn_a_log[l],
                             gdn_dt_bias[l], gdn_norm_w[l], lru_conv_w[l], lru_conv_b[l],
                             lru_wa[l], lru_ba[l], lru_wx[l], lru_bx[l], lru_lambda[l], w_out[l])
        x = x + memory_cross_attention(rmsnorm(x, norm_xattn_w[l]), rmsnorm(mem, norm_mem_w[l]),
                                       xattn_wq[l], xattn_wkv[l], xattn_wo[l])
        x = x + peer_ffn(rmsnorm(x, norm_ffn_w[l]), peer_wq[l], peer_subkeys[l], peer_u[l], peer_v[l])
    return rmsnorm(x, norm_final_w)


def setup_inputs(seed=0):
    out = dict(first_inputs(seed))
    for name, value in second_inputs(seed + 1).items():
        if name != "x":
            out[name + "_2"] = value
    return out


def reference(
    x, meta_tokens, w_in, w_ret_o, w_att_o, w_mix_o, w_ff1, w_ff2, norm_mix_pre, norm_mix_post,
    norm_ff_pre, norm_ff_post, ret_decay, attn_sink, mem_2, norm_mix_w_2, w_in_2, conv_qkv_w_2,
    gdn_a_log_2, gdn_dt_bias_2, gdn_norm_w_2, lru_conv_w_2, lru_conv_b_2, lru_wa_2, lru_ba_2,
    lru_wx_2, lru_bx_2, lru_lambda_2, w_out_2, norm_xattn_w_2, norm_mem_w_2, xattn_wq_2,
    xattn_wkv_2, xattn_wo_2, norm_ffn_w_2, peer_wq_2, peer_subkeys_2, peer_u_2, peer_v_2,
    norm_final_w_2,
):
    x = first_block(
        x, meta_tokens, w_in, w_ret_o, w_att_o, w_mix_o, w_ff1, w_ff2, norm_mix_pre,
        norm_mix_post, norm_ff_pre, norm_ff_post, ret_decay, attn_sink,
    )
    return second_block(
        x, mem_2, norm_mix_w_2, w_in_2, conv_qkv_w_2, gdn_a_log_2, gdn_dt_bias_2, gdn_norm_w_2,
        lru_conv_w_2, lru_conv_b_2, lru_wa_2, lru_ba_2, lru_wx_2, lru_bx_2, lru_lambda_2,
        w_out_2, norm_xattn_w_2, norm_mem_w_2, xattn_wq_2, xattn_wkv_2, xattn_wo_2,
        norm_ffn_w_2, peer_wq_2, peer_subkeys_2, peer_u_2, peer_v_2, norm_final_w_2,
    )


_drawn_inputs = setup_inputs


def setup_inputs(seed=0):
    import zlib

    import numpy as np

    out = dict(_drawn_inputs(seed))
    spreads = {}
    factors = {'attn_sink': 8.0,
     'gdn_norm_w_2': 5.519,
     'lru_conv_b_2': 5.298,
     'lru_ba_2': 8.0,
     'lru_bx_2': 8.0,
     'norm_xattn_w_2': 8.0,
     'norm_mem_w_2': 8.0,
     'norm_ffn_w_2': 10.461}
    for name, (base, spread) in spreads.items():
        noise = np.random.default_rng([zlib.crc32(name.encode()), seed]).standard_normal(out[name].shape)
        drawn = base * np.exp(spread * noise) if base else spread * noise
        out[name] = __import__('jax').numpy.asarray(drawn.astype(out[name].dtype))
    for name, factor in factors.items():
        out[name] = (out[name] * factor).astype(out[name].dtype)
    return out
```

```python
import concourse.bass as bass
from concourse import mybir
from contextlib import ExitStack

D, TT, NM, SL = 1024, 528, 16, 2048
C_OFF, N = {}, 0
for _n, _w in [("ident", 128), ("ones", 128), ("onesm", 128), ("eps", 1), ("permR", 128), ("permA", 128),
               ("cosR", 528), ("sinR", 528), ("cosA", 528), ("sinA", 528), ("rel", 928),
               ("mA", 400), ("mB", 272), ("mC", 144)]:
    C_OFF[_n] = (N, _w)
    N += _w
C_W = N
C2_OFF, N = {}, 0
for _n, _w in [("triu", 128), ("negL", 128), ("negU", 128), ("lev", 7 * 128), ("iota", 128)]:
    C2_OFF[_n] = (N, _w)
    N += _w
C2_W = N
JT = [(0, 16)] + [(16 + 128 * j, 128) for j in range(4)]


def activation(*a, **k):
    return lambda e: e.activation(*a, **k)


def match_replace(*a, **k):
    return lambda e: e.match_replace(*a, **k)


def matmul(*a, **k):
    return lambda e: e.matmul(*a, **k)


def max8(*a, **k):
    return lambda e: e.max(*a, **k)


def max_index(*a, **k):
    return lambda e: e.max_index(*a, **k)


def memset(*a, **k):
    return lambda e: e.memset(*a, **k)


def reciprocal(*a, **k):
    return lambda e: e.reciprocal(*a, **k)


def scalar_tensor_tensor(*a, **k):
    return lambda e: e.scalar_tensor_tensor(*a, **k)


def tensor_copy(*a, **k):
    return lambda e: e.tensor_copy(*a, **k)


def tensor_reduce(*a, **k):
    return lambda e: e.tensor_reduce(*a, **k)


def tensor_scalar(*a, **k):
    return lambda e: e.tensor_scalar(*a, **k)


def tensor_tensor(*a, **k):
    return lambda e: e.tensor_tensor(*a, **k)


def tensor_tensor_scan(*a, **k):
    return lambda e: e.tensor_tensor_scan(*a, **k)


def transpose(*a, **k):
    return lambda e: e.transpose(*a, **k)


def program(nc, A, out, stage):
    F, U32 = mybir.dt.float32, mybir.dt.uint32
    ALU, ACT, AX = mybir.AluOpType, mybir.ActivationFunctionType, mybir.AxisListType
    MUL, ADD, SUB, MAX, MIN = ALU.mult, ALU.add, ALU.subtract, ALU.max, ALU.min

    ctx = ExitStack()
    with ctx:
        M = ctx.enter_context(nc.sbuf_tensor("M", [128, 52600], F))
        PSM = ctx.enter_context(nc.psum_tensor("PSM", [128, 8, 512], F))

        class Queue:

            def __init__(self, name):
                self.sem = ctx.enter_context(nc.semaphore("s_" + name))
                self.n, self.ops, self.met = 0, [], {}

            def wait(self, toks):
                for t in toks:
                    if t is None:
                        continue
                    if isinstance(t, list):
                        self.wait(t)
                        continue
                    s, v = t
                    if self.met.get(s.name, 0) < v:
                        self.met[s.name] = v
                        self.ops.append(lambda e, s=s, v=v: e.wait_ge(s, v))

            def do(self, f, *toks):
                self.wait(toks)
                self.n += 1
                self.ops.append(lambda e: f(e).then_inc(self.sem, 1))
                return (self.sem, self.n)

            def quiet(self, f, *toks):
                self.wait(toks)
                self.ops.append(f)

            def last(self):
                return (self.sem, self.n) if self.n else None

        P, V, S, G, Y = (Queue(n) for n in ("pe", "dve", "act", "pool", "sp"))

        def now():
            return [q.last() for q in (P, V, S, G)]

        dma_count = {}

        def load(q, sem, dst, src, *toks):
            dma_count[sem.name] = dma_count.get(sem.name, 0) + 16
            q.quiet(lambda e: e.dma_start(dst, src).then_inc(sem, 16), *toks)
            return (sem, dma_count[sem.name])

        def newsem(name):
            return ctx.enter_context(nc.semaphore(name))

        class Ring:

            def __init__(self, bufs):
                self.bufs, self.free, self.i = bufs, [[] for _ in bufs], -1

            def take(self):
                self.i = (self.i + 1) % len(self.bufs)
                return self.bufs[self.i], self.i, self.free[self.i]

        at = [0]

        def place(n):
            a = at[0]
            at[0] += n
            assert at[0] <= 52600, at[0]
            return a

        oH = place(8 * TT)
        oU = place(8 * TT)
        oW = place(6 * SL)
        oC = place(C_W)
        oVec = place(4 * 8 * 2 + 2 * 8 + 2 * 16)
        oVec2 = place(130)
        oZ = at[0]

        def sb(off, n):
            return M[:, off:off + n]

        hT = [sb(oH + k * TT, TT) for k in range(8)]
        uT = [sb(oU + k * TT, TT) for k in range(8)]
        con = {n: M[:, oC + o:oC + o + w] for n, (o, w) in C_OFF.items()}
        eps = con["eps"]

        s_c = newsem("s_c")
        t_con = load(S, s_c, sb(oC, C_W), A["consts"])
        t_con = load(S, s_c, sb(oVec, 112), A["vec1"])
        t_con = load(S, s_c, sb(oVec2, 129), A["vec2"])
        s_h = newsem("s_h")
        t_h = load(Y, s_h, M[:, oH:oH + 8 * TT], A["hin"])

        def vec(i, k):
            return M[:, oVec + i * 8 + k:oVec + i * 8 + k + 1]

        wsem = [newsem(f"s_w{i}") for i in range(8)]
        wring = Ring([sb(oW + i * SL, SL) for i in range(6)])

        def chunk(src):
            b, i, free = wring.take()
            return b, i, load(Y, wsem[i], b, src, free)

        pring = Ring([0, 2, 4, 6])

        def pv(b, T, rows=128):
            return PSM[0:rows, b:b + 2, 0:264] if T == TT else PSM[0:rows, b, 0:T]

        def fv(ap, T):
            return ap.rearrange("p (a b) -> p a b", a=2) if T == TT else ap

        def gemm(b, lhs, rhs, T, toks, rows=128):
            P.wait(toks)
            segs = [(0, 0, 264), (1, 264, 528)] if T == TT else [(0, 0, T)]
            n = len(lhs)
            for s, lo, hi in segs:
                for k in range(n):
                    f = (matmul(PSM[0:rows, b + s, 0:hi - lo], lhs[k], rhs[k][:, lo:hi],
                                  start=(k == 0), stop=(k == n - 1)))
                    if s == segs[-1][0] and k == n - 1:
                        return P.do(f)
                    P.quiet(f)

        def rms_rstd(tiles, T, rs, sqs, scale, tok, n=8):
            b, pi, free = pring.take()
            P.wait([free, t_con])
            for k in range(n):
                sq, si, sf = sqs.take()
                ts = S.do(activation(sq[:, 0:T], tiles[k], ACT.Square), tok, sf)
                tp = accumulate(b, con["ones"], sq, T, k, n, ts)
                sqs.free[si] = [tp]
            return finish_rstd(b, pi, T, rs, scale, tp)

        def accumulate(b, lhs, rhs, T, k, n, tok):
            P.wait([tok])
            segs = [(0, 0, 264), (1, 264, 528)] if T == TT else [(0, 0, T)]
            for s, lo, hi in segs:
                f = (matmul(PSM[:, b + s, 0:hi - lo], lhs, rhs[:, lo:hi],
                              start=(k == 0), stop=(k == n - 1), skip_group_check=True))
                if s == segs[-1][0]:
                    return P.do(f)
                P.quiet(f)

        def finish_rstd(b, pi, T, rs, scale, tp):
            t1 = S.do(activation(fv(rs[:, 0:T], T), pv(b, T), ACT.Ln, bias=eps, scale=scale), tp)
            pring.free[pi] = [t1]
            return S.do(activation(rs[:, 0:T], rs[:, 0:T], ACT.Exp, scale=-0.5), t1)

        def scaled(dst, src, w, rs, T, tok):
            for k in range(8):
                t = V.do(scalar_tensor_tensor(out=dst[k], in0=src[k], scalar=w(k),
                                                               in1=rs[:, 0:T], op0=MUL, op1=MUL), tok)
            return t

        def post_norm_add(y, w, c0, T, rs, toks):
            for k in range(8):
                t = V.do(scalar_tensor_tensor(out=y[k][:, c0:], in0=y[k][:, c0:], scalar=w(k),
                                                               in1=rs[:, 0:T], op0=MUL, op1=MUL), toks)
                t = V.do(tensor_tensor(hT[k][:, c0:], hT[k][:, c0:], y[k][:, c0:], ADD), t)
            return t

        def columns(nchunks, src, consume, rhs, lo, n, tok, kk=8):
            o = 0
            for c in range(nchunks):
                b0, wslot, tw = src(c)
                w = b0.rearrange("p (k n) -> p k n", k=kk)
                P.wait([tw])
                for a in range(w.shape[2] // 128):
                    b, pi, free = pring.take()
                    tp = gemm(b, [w[:, k, 128 * a:128 * a + 128] for k in range(kk)],
                              [r[:, lo:] for r in rhs], n, [free, tok])
                    pring.free[pi] = consume(o, b, tp)
                    o += 1
                wring.free[wslot] = [tp]

        at[0] = oZ
        oQR, oKR, oV, oG = place(4 * TT), place(4 * TT), place(5 * 1024), place(8 * TT)
        oQA, oKA, oVA, oOA = place(4 * TT), place(TT), place(5 * 128), place(4 * TT)
        oX = at[0]
        qr = [sb(oQR + k * TT, TT) for k in range(4)]
        kr = [sb(oKR + k * TT, TT) for k in range(4)]
        gR = [sb(oG + k * TT, TT) for k in range(8)]
        qa = [sb(oQA + k * TT, TT) for k in range(4)]
        oa = [sb(oOA + k * TT, TT) for k in range(4)]
        ka = sb(oKA, TT)
        vR = M[:, oV:oV + 5120].rearrange("p (j n) -> p j n", j=5)
        vA = M[:, oVA:oVA + 640].rearrange("p (j n) -> p j n", j=5)
        gate_r = [sb(oQR + k * TT, TT) for k in range(8)]
        gate_a = [sb(oV + k * TT, TT) for k in range(8)]
        hid = [sb(oZ + k * TT, TT) for k in range(32)]

        free_scratch = 52600 - oX

        def layer(l, t_in):
            c0 = 16 * l
            T = TT - c0
            sqs = Ring([sb(oX + i * TT, TT) for i in range(3)])
            rs = sb(oX + 3 * TT, TT)
            enter = now()
            S.wait(enter)
            V.wait(enter)
            G.wait(enter)
            t_rs = rms_rstd([h[:, :] for h in hT], TT, rs, sqs, 1.0 / D, t_in)
            t_u = scaled(uT, hT, lambda k: vec(4 * l + 0, k), rs, TT, t_rs)

            rx = Ring([sb(oX + (4 + i) * TT, TT) for i in range(3)])
            ry = Ring([sb(oX + (7 + i) * TT, TT) for i in range(2)])
            w_in = A["w_in"]
            wi = [0]

            def next_in():
                c = chunk(w_in[l, wi[0]])
                wi[0] += 1
                return c[0].rearrange("p (k n) -> p k n", k=8), c[1], c[2]

            def rotated(w, half, dst, perm, cos, sin, lo):
                n = TT - lo
                b, pi, free = pring.take()
                tp = gemm(b, [w[:, k, half] for k in range(8)], [u[:, lo:] for u in uT], n, [free, t_u])
                x, xi, xf = rx.take()
                tx = S.do(activation(fv(x[:, 0:n], n), pv(b, n), ACT.Copy), tp, xf)
                pring.free[pi] = [tx]

                def rest():
                    b2, pi2, free2 = pring.take()
                    tp2 = gemm(b2, [con[perm]], [x[:, 0:n]], n, [free2, tx])
                    y, yi, yf = ry.take()
                    tv = V.do(tensor_tensor(fv(y[:, 0:n], n), pv(b2, n), fv(con[sin][:, lo:], n), MUL),
                              tp2, yf)
                    pring.free[pi2] = [tv]
                    tg = G.do(tensor_tensor(dst[:, lo:], x[:, 0:n], con[cos][:, lo:], MUL), tx)
                    ta = V.do(tensor_tensor(dst[:, lo:], dst[:, lo:], y[:, 0:n], ADD), tv, tg)
                    rx.free[xi] = [tp2, tg]
                    ry.free[yi] = [ta]
                    return ta
                return tp, rest

            pend = []

            def rot(*a):
                tp, rest = rotated(*a)
                pend.append(rest)
                if len(pend) > 1:
                    res.append(pend.pop(0)())
                return tp

            res = []
            for base, lo in ((qr, c0), (kr, 0)):
                for c in range(2):
                    w, wslot, tw = next_in()
                    P.wait([tw])
                    for a in range(2):
                        tp = rot(w, slice(128 * a, 128 * a + 128), base[2 * c + a], "permR", "cosR", "sinR", lo)
                    wring.free[wslot] = [tp]
            for c in range(2):
                w, wslot, tw = next_in()
                P.wait([tw])
                for a in range(2):
                    tp = rot(w, slice(128 * a, 128 * a + 128), qa[2 * c + a], "permA", "cosA", "sinA", c0)
                wring.free[wslot] = [tp]
            w, wslot, tw = next_in()
            P.wait([tw])
            rot(w, slice(0, 128), ka, "permA", "cosA", "sinA", 0)
            t_vs = []

            def tokens(w, cols, dst):
                n = cols.stop - cols.start
                for j, (j0, nj) in enumerate(JT):
                    b, pi, free = pring.take()
                    tp = gemm(b, [u[:, j0:j0 + nj] for u in uT], [w[:, k, cols] for k in range(8)], n,
                              [free, t_u], rows=nj)
                    q = S if j % 2 else V
                    f = ((activation(dst(j, nj), PSM[0:nj, b, 0:n], ACT.Copy)) if j % 2
                         else (tensor_copy(dst(j, nj), PSM[0:nj, b, 0:n])))
                    tv = q.do(f, tp)
                    pring.free[pi] = [tv]
                    t_vs.append(tv)
                return tp

            wring.free[wslot] = [tokens(w, slice(128, 256), lambda j, nj: vA[0:nj, j, :])]
            res.append(pend.pop(0)())
            for c in range(4):
                w, wslot, tw = next_in()
                P.wait([tw])
                wring.free[wslot] = [tokens(w, slice(0, 256),
                                            lambda j, nj, c=c: vR[0:nj, j, 256 * c:256 * c + 256])]
            t_v = [V.last(), S.last()]

            def in_chunk(_):
                c = chunk(w_in[l, wi[0]])
                wi[0] += 1
                return c

            t_g = []

            def silu(o, b, tp):
                t = S.do(activation(fv(gR[o][:, c0:], T), pv(b, T), ACT.Silu), tp)
                t_g.append(t)
                return [t]
            columns(4, in_chunk, silu, uT, c0, T, None)
            t_rot = V.last()
            if stage == 11:
                return [t_rot, S.last()]

            enter = now()
            V.wait(enter)
            S.wait(enter)
            G.wait(enter)
            DT = Ring([sb(oX + i * 928, 928) for i in range(2)])
            sd = Ring([sb(oX + 1856 + i * TT, TT) for i in range(6)])
            oS = Ring([sb(oX + 1856 + (6 + i) * TT, TT) for i in range(3)])
            assert 1856 + 9 * TT <= free_scratch, free_scratch
            sq2 = Ring([uT[0][:, :]])
            lgo = oVec + 80 + 16 * l
            lg = lambda d, h: M[:, lgo + 8 * d + h:lgo + 8 * d + h + 1]
            if l == 0:
                lgall = M[:, oVec + 80:oVec + 112]
                t_lg = S.do(activation(lgall, lgall, ACT.Exp), t_con)
                for i in range(4):
                    ap = M[:, oVec + 80 + 8 * i:oVec + 88 + 8 * i]
                    if i % 2 == 0:
                        t_lg0[0] = V.do(tensor_scalar(ap, ap, -1.0, None, MUL), t_lg)
            st = {}

            def r_a(h):
                dt, di, df = DT.take()
                t0 = V.do(tensor_scalar(dt, con["rel"], lg(0, h), None, MUL), df, t_lg0[0])
                t1 = V.do(scalar_tensor_tensor(out=dt, in0=con["rel"], scalar=lg(1, h), in1=dt,
                                                           op0=MUL, op1=MIN), t0)
                te = S.do(activation(dt, dt, ACT.Exp), t1)
                a, p0 = h // 2, 64 * (h % 2)
                outs = []
                for j, (j0, nj) in enumerate(JT):
                    b, pi, free = pring.take()
                    tp = gemm(b, [kr[a][p0:p0 + 64, j0:j0 + nj]], [qr[a][p0:p0 + 64, c0:]], T, [free, t_rot], rows=nj)
                    s, si, sf = sd.take()
                    win = dt[0:nj, c0 - j0 + 400:c0 - j0 + 400 + T]
                    tv = V.do(scalar_tensor_tensor(
                        out=fv(s[0:nj, 0:T], T), in0=pv(b, T, nj), scalar=0.125, in1=fv(win, T),
                        op0=MUL, op1=MUL), tp, te, sf)
                    pring.free[pi] = [tv]
                    outs.append((s, si, tv))
                DT.free[di] = [outs[-1][2]]
                b, pi, free = pring.take()
                P.wait([free, t_v])
                for j, (j0, nj) in enumerate(JT):
                    s, si, tv = outs[j]
                    tp = accumulate(b, vR[0:nj, j, 128 * h:128 * h + 128], s[0:nj, :], T, j, 5, tv)
                    sd.free[si] = [tp]
                o, oi, of = oS.take()
                t = S.do(activation(fv(o[:, 0:T], T), pv(b, T), ACT.Copy), tp, of)
                pring.free[pi] = [t]
                st[h] = (o, oi, t)

            def r_c(h):
                o, oi, t = st[h]
                b, pi, free = pring.take()
                tp = gemm(b, [con["onesm"]], [o[:, 0:T]], T, [free, t])
                tv = V.do(scalar_tensor_tensor(out=fv(o[:, 0:T], T), in0=pv(b, T), scalar=-1.0,
                                                           in1=fv(o[:, 0:T], T), op0=MUL, op1=ADD), tp)
                pring.free[pi] = [tv]
                s, si, sf = sq2.take()
                ts = S.do(activation(s[:, 0:T], o[:, 0:T], ACT.Square), tv, sf)
                st[h] = (o, oi, tv, s, si, ts)

            def r_d(h):
                o, oi, tv, s, si, ts = st[h]
                b, pi, free = pring.take()
                tp = gemm(b, [con["onesm"]], [s[:, 0:T]], T, [free, ts])
                t = finish_rstd(b, pi, T, s, 1.0, tp)
                t = V.do(tensor_tensor(o[:, 0:T], o[:, 0:T], s[:, 0:T], MUL), t)
                sq2.free[si] = [t]
                t = G.do(tensor_tensor(gR[h][:, c0:], gR[h][:, c0:], o[:, 0:T], MUL), t)
                oS.free[oi] = [t]
                t_ret.append(t)

            t_ret = []
            sq2 = Ring([sb(oX + 1856 + (9 + i) * TT, TT) for i in range(1)])
            assert 1856 + 10 * TT <= free_scratch, free_scratch
            for h in range(8 + 2):
                if h < 8:
                    r_a(h)
                if h >= 2:
                    r_d(h - 2)
                if 1 <= h < 9:
                    r_c(h - 1)

            enter = now()
            V.wait(enter)
            S.wait(enter)
            G.wait(enter)
            sc_r = Ring([sb(oX + i * 408, 408) for i in range(4)])
            pt_r = Ring([sb(oX + 1632 + i * 512, 512) for i in range(3)])
            tiny = Ring([sb(oX + 1632 + 1536 + i * 4, 4) for i in range(4)])
            so = oVec + 64 + 8 * l
            units = []
            for a in range(4):
                for n in ([-1] if l == 0 else []) + [0, 1, 2, 3]:
                    for half in range(2):
                        units.append((a, n, half))
            obank = {}
            av = {}

            def shape(n):
                if n < 0:
                    return 0, 16, [(0, 144)], con["mC"], [1]
                q0 = 16 + 128 * n
                blocks = [m for m in (n - 1, n, n + 1) if 0 <= m < 4]
                lo, hi = 16 + 128 * blocks[0], 16 + 128 * (blocks[-1] + 1)
                if n == 0:
                    return q0, 128, [(0, hi)], con["mB"], [m + 1 for m in blocks]
                return q0, 128, [(0, 16), (lo, hi)], con["mA"], [m + 1 for m in blocks]

            def a_scores(u):
                a, n, half = units[u]
                h = a + 4 * half
                p0 = 64 * half
                q0, nq, ks, mask, blk = shape(n)
                b, pi, free = pring.take()
                P.wait([free, t_rot])
                o = 0
                for lo, hi in ks:
                    f = (matmul(
                        PSM[0:nq, b, o:o + hi - lo], qa[a][p0:p0 + 64, q0:q0 + nq], ka[p0:p0 + 64, lo:hi],
                        start=True, stop=True, skip_group_check=True))
                    tp = P.do(f)
                    o += hi - lo
                s, si, sf = sc_r.take()
                y, yi, yf = tiny.take()
                tg = G.do(tensor_copy(s[0:nq, o:o + 1], M[0:nq, so + h:so + h + 1]), sf)
                tv = V.do(scalar_tensor_tensor(out=s[0:nq, 0:o], in0=PSM[0:nq, b, 0:o], scalar=0.125,
                                                           in1=mask[0:nq, 0:o], op0=MUL, op1=ADD), tp, sf)
                pring.free[pi] = [tv]
                tm = V.do(tensor_reduce(y[0:nq, 0:1], s[0:nq, 0:o + 1], AX.X, MAX, negate=True),
                          tv, tg, yf)
                te = S.do(activation(s[0:nq, 0:o + 1], s[0:nq, 0:o + 1], ACT.Exp, bias=y[0:nq, 0:1],
                                                 accum_out=y[0:nq, 1:2]), tm)
                tr = V.do(reciprocal(y[0:nq, 2:3], y[0:nq, 1:2]), te)
                tn = V.do(tensor_scalar(s[0:nq, 0:o], s[0:nq, 0:o], y[0:nq, 2:3], None, MUL), tr)
                tiny.free[yi] = [tn]
                av[u] = (s, si, tn)

            def a_turn(u):
                a, n, half = units[u]
                s, si, tn = av[u]
                q0, nq, ks, mask, blk = shape(n)
                b, pi, free = pring.take()
                P.wait([free, tn])
                P.quiet(transpose(PSM[0:16, b + 1, 0:nq], s[0:nq, 0:16], con["ident"][0:nq, 0:nq]))
                for i in range(len(blk)):
                    f = transpose(PSM[:, b, 128 * i:128 * i + nq],
                                                   s[0:nq, 16 + 128 * i:144 + 128 * i], con["ident"][0:nq, 0:nq])
                    tp = P.do(f)
                sc_r.free[si] = [tp]
                pt, ti, tf = pt_r.take()
                nb = len(blk)
                t1 = V.do(tensor_copy(pt[0:16, 0:nq], PSM[0:16, b + 1, 0:nq]), tp, tf)
                src = PSM[:, b, 0:128 * nb].rearrange("p (i q) -> p i q", q=128)[:, :, 0:nq]
                dst = pt[:, 128:128 + 128 * nb].rearrange("p (i q) -> p i q", q=128)[:, :, 0:nq]
                t2 = S.do(activation(dst, src, ACT.Copy), tp, tf)
                pring.free[pi] = [t1, t2]
                av[u] = (pt, ti, [t1, t2])

            def a_out(u, oring):
                a, n, half = units[u]
                pt, ti, tok = av[u]
                q0, nq, ks, mask, blk = shape(n)
                p0 = 64 * half
                if a not in obank:
                    b, pi, free = oring.take()
                    obank[a] = (b, pi)
                    P.wait([free])
                b, pi = obank[a]
                dst = PSM[p0:p0 + 64, b + 1, 0:16] if n < 0 else PSM[p0:p0 + 64, b, 128 * n:128 * n + 128]
                P.wait([tok, t_v])
                P.quiet(matmul(dst, vA[0:16, 0, 64 * half:64 * half + 64], pt[0:16, 0:nq],
                                           start=True, stop=False, skip_group_check=True))
                for i, m in enumerate(blk):
                    f = matmul(dst, vA[:, m, 64 * half:64 * half + 64],
                                                     pt[:, 128 + 128 * i:128 + 128 * i + nq], start=False,
                                                     stop=(i == len(blk) - 1), skip_group_check=True)
                    tp = P.do(f)
                pt_r.free[ti] = [tp]
                if n == 3 and half == 1:
                    t = S.do(activation(oa[a][:, 16:], PSM[:, b, 0:512], ACT.Copy), tp)
                    if l == 0:
                        t = S.do(activation(oa[a][:, 0:16], PSM[:, b + 1, 0:16], ACT.Copy), tp)
                    oring.free[pi] = [t]

            oring = Ring([pring.bufs.pop()])
            oring.free = [pring.free.pop()]
            pring.i = -1
            for u in range(len(units) + 4):
                if u < len(units):
                    a_scores(u)
                if 2 <= u < len(units) + 2:
                    a_turn(u - 2)
                if u >= 3 and u - 3 < len(units):
                    a_out(u - 3, oring)
            pring.bufs.append(oring.bufs[0])
            pring.free.append(oring.free[0])
            if stage == 12:
                return now()

            enter = now()
            S.wait(enter)
            V.wait(enter)
            G.wait(enter)
            for g in (gate_r, gate_a):
                def sigm(o, b, tp, g=g):
                    return [S.do(activation(fv(g[o][:, c0:], T), pv(b, T), ACT.Sigmoid), tp)]
                columns(4, in_chunk, sigm, uT, c0, T, None)
            t_gate = S.last()

            def into(g):
                def f(o, b, tp):
                    return [V.do(tensor_tensor(fv(g[o][:, c0:], T), pv(b, T), fv(g[o][:, c0:], T), MUL),
                                 tp, t_gate)]
                return f
            columns(4, lambda c: chunk(A["w_ret_o"][l, c]), into(gate_r), gR, c0, T, enter)
            columns(2, lambda c: chunk(A["w_att_o"][l, c]), into(gate_a), oa, c0, T, enter, kk=4)
            t = V.last()
            for k in range(8):
                t_m = G.do(tensor_tensor(gate_r[k][:, c0:], gate_r[k][:, c0:], gate_a[k][:, c0:], ADD), t)
            finish(lambda c: chunk(A["w_mix_o"][l, c]), 4, gate_r, 8, c0, T, 4 * l + 1, t_m, enter)
            if stage == 13:
                return now()

            enter = now()
            if l == 1:
                P.wait([load(Y, s_c2, sb(oC + 385, C2_W), A["consts2"], enter)])
            S.wait(enter)
            V.wait(enter)
            G.wait(enter)
            sqs = Ring([sb(oX + i * TT, TT) for i in range(3)])
            rs = sb(oX + 3 * TT, TT)
            t_rs = rms_rstd([h[:, c0:] for h in hT], T, rs, sqs, 1.0 / D, enter)
            t_u = scaled([u[:, c0:] for u in uT], [h[:, c0:] for h in hT], lambda k: vec(4 * l + 2, k), rs, T, t_rs)

            def relu2(o, b, tp):
                t = S.do(activation(fv(hid[o][:, c0:], T), pv(b, T), ACT.Relu), tp)
                G.do(tensor_tensor(hid[o][:, c0:], hid[o][:, c0:], hid[o][:, c0:], MUL), t)
                return [t]
            columns(16, lambda c: chunk(A["w_ff1"][l, c]), relu2, uT, c0, T, t_u)
            finish(lambda c: chunk(A["w_ff2"][l, c]), 16, hid, 32, c0, T, 4 * l + 3, G.last(), now())
            return now()

        def finish(src, nchunks, rhs, K, c0, T, w, tok, enter):
            S.wait([enter])
            V.wait([enter])
            sqs = Ring([sb(oX + i * TT, TT) for i in range(3)])
            rs = sb(oX + 3 * TT, TT)
            nb = pring.bufs.pop()
            nfree = pring.free.pop()
            pring.i = -1
            P.wait(nfree)
            pend = []

            def one(o, b, pi, tp):
                t1 = V.do(tensor_copy(fv(uT[o][:, c0:], T), pv(b, T)), tp)
                s, si, sf = sqs.take()
                t2 = S.do(activation(s[:, 0:T], uT[o][:, c0:], ACT.Square), t1, sf)
                pring.free[pi] = [t1]
                if pend:
                    pend.pop()()

                def later():
                    sqs.free[si] = [accumulate(nb, con["ones"], s, T, o, 8, t2)]
                pend.append(later)

            if K == 32:
                for o in range(8):
                    ws = [chunk_of(src(2 * o + i)) for i in range(2)]
                    b, pi, free = pring.take()
                    lhs = [ws[k // 16][0][:, 128 * (k % 16):128 * (k % 16) + 128] for k in range(32)]
                    tp = gemm(b, lhs, [r[:, c0:] for r in rhs], T, [free, tok, ws[0][2], ws[1][2]])
                    for x in ws:
                        wring.free[x[1]] = [tp]
                    one(o, b, pi, tp)
            else:
                for c in range(nchunks):
                    b0, wslot, tw = src(c)
                    wv = b0.rearrange("p (k n) -> p k n", k=8)
                    for a in range(2):
                        b, pi, free = pring.take()
                        tp = gemm(b, [wv[:, k, 128 * a:128 * a + 128] for k in range(8)],
                                  [r[:, c0:] for r in rhs], T, [free, tok, tw])
                        one(2 * c + a, b, pi, tp)
                    wring.free[wslot] = [tp]
            pend.pop()()
            pring.bufs.append(nb)
            pring.free.append([])
            t = finish_rstd(nb, len(pring.bufs) - 1, T, rs, 1.0 / D, P.last())
            post_norm_add(uT, lambda k: vec(w, k), c0, T, rs, [t, V.last()])

        def chunk_of(c):
            return c

        T2 = 512
        xT = [h[:, 16:] for h in hT]
        uX = [u[:, 16:] for u in uT]
        c2 = {n: M[:, oC + 385 + o:oC + 385 + o + w] for n, (o, w) in C2_OFF.items()}
        s_c2 = newsem("s_c2")

        def v2(o, n=1):
            return M[:, oVec2 + o:oVec2 + o + n]

        def fence():
            e = now()
            for q in (V, S, G):
                q.wait(e)
            return e

        def pairmul(q, dst, a, b, op=MUL, *toks):
            return q.do(tensor_tensor(dst, a, b, op), *toks)

        def norm_in(w0, tok):
            sqs = Ring([sb(oNs + i * 512, 512) for i in range(3)])
            rs = sb(oNs + 1536, 512)
            t_rs = rms_rstd(xT, T2, rs, sqs, 1.0 / D, tok)
            return scaled(uX, xT, lambda k: v2(w0 + k), rs, T2, t_rs)

        def add_in(o, b, tp):
            return [V.do(tensor_tensor(xT[o], PSM[:, b, 0:T2], xT[o], ADD), tp)]

        oNs = 52600 - 2048

        def mixer():
            at[0] = oZ
            oq, ok, ov, oz, oxr, ogt = (place(2048) for _ in range(6))
            okt, ovt, oat, owt, ost, ot = place(2048), place(2048), place(2048), place(2048), place(512), place(416)
            oT = at[0]
            q = [sb(oq + i * 512, 512) for i in range(4)]
            k = [sb(ok + i * 512, 512) for i in range(4)]
            v = [sb(ov + i * 512, 512) for i in range(4)]
            z = [sb(oz + i * 512, 512) for i in range(4)]
            xr = [sb(oxr + i * 512, 512) for i in range(4)]
            gt = [sb(ogt + i * 512, 512) for i in range(4)]
            ktm = [sb(okt + i * 512, 512) for i in range(4)]
            vtm = [sb(ovt + i * 512, 512) for i in range(4)]
            XT = [sb(ov + i * 512, 512) for i in range(4)]
            atn = [sb(oat + i * 512, 512) for i in range(4)]
            nwT = [sb(owt + i * 512, 512) for i in range(4)]
            st = sb(ost, 512)
            wab = sb(ot, 64)
            g, beta, gc, ngc, gl, egc, bg, dl, el, tm1, tm2 = (sb(ot + 64 + 16 * i, 16) for i in range(11))
            ea, c8, nc8, lt = (sb(ot + 240 + 8 * i, 8) for i in range(4))
            e0 = fence()
            s_ab = newsem("s_ab")
            t_ab = load(Y, s_ab, wab, A["w_ab"], e0)
            owl = oat
            t_wl = load(Y, s_ab, sb(owl, 1024), A["w_lru"], e0)
            t_u = norm_in(0, e0)

            b, pi, free = pring.take()
            P.wait([free, t_u, t_ab, t_wl])
            for j in range(4):
                for kk in range(8):
                    f = matmul(PSM[:, b, 8 * j:8 * j + 8], uX[kk][:, 128 * j:128 * j + 128],
                                                       wab[:, 8 * kk:8 * kk + 8], start=(kk == 0), stop=(kk == 7),
                                                       skip_group_check=True)
                    tp = P.do(f)
            ab = PSM[:, b, 0:32].rearrange("p (j n) -> p j n", n=8)
            c44 = lambda ap: ap.rearrange("p (j n) -> p j n", n=4)
            t = V.do(tensor_tensor(c44(tm1), ab[:, :, 0:4], v2(125, 4).unsqueeze(1).to_broadcast([128, 4, 4]), ADD), tp)
            tb = S.do(activation(c44(beta), ab[:, :, 4:8], ACT.Sigmoid), t)
            pring.free[pi] = [t, tb]
            t = V.do(scalar_tensor_tensor(out=tm2, in0=tm1, scalar=-1.0, in1=tm1, op0=MUL, op1=MAX), t)
            t = S.do(activation(tm2, tm2, ACT.Exp, scale=-1.0), t)
            t = S.do(activation(tm2, tm2, ACT.Ln, bias=con["ones"][:, 0:1]), t)
            t2 = S.do(activation(ea[:, 0:4], v2(121, 4), ACT.Exp), t)
            t = V.do(scalar_tensor_tensor(out=tm1, in0=tm1, scalar=0.0, in1=tm2, op0=MAX, op1=ADD), t2)
            t = V.do(scalar_tensor_tensor(out=c44(g), in0=c44(tm1), scalar=-1.0,
                                                      in1=ea[:, 0:4].unsqueeze(1).to_broadcast([128, 4, 4]),
                                                      op0=MUL, op1=MUL), t)
            b, pi, free = pring.take()
            P.wait([free])
            P.do(matmul(PSM[:, b, 0:16], c2["triu"], g, start=True, stop=True, skip_group_check=True), t)
            tp = P.do(matmul(PSM[:, b, 16:32], con["ones"], g, start=True, stop=True,
                                         skip_group_check=True), t)
            t = V.do(tensor_copy(gc, PSM[:, b, 0:16]), tp)
            t = V.do(tensor_copy(gl, PSM[:, b, 16:32]), tp)
            pring.free[pi] = [t]
            t1 = V.do(tensor_scalar(ngc, gc, -1.0, None, MUL), t)
            t2 = V.do(tensor_tensor(dl, gl, gc, SUB), t)
            t3 = S.do(activation(egc, gc, ACT.Exp), t)
            S.do(activation(dl, dl, ACT.Exp), t2)
            t4 = S.do(activation(el, gl, ACT.Exp), t)
            t_gates = V.do(tensor_tensor(bg, beta, egc, MUL), t3, tb, t4)

            lam = v2(116, 4)
            t = V.do(scalar_tensor_tensor(out=lt[:, 0:4], in0=lam, scalar=-1.0, in1=lam, op0=MUL, op1=MAX))
            t = S.do(activation(lt[:, 0:4], lt[:, 0:4], ACT.Exp, scale=-1.0), t)
            t = S.do(activation(lt[:, 0:4], lt[:, 0:4], ACT.Ln, bias=con["ones"][:, 0:1]), t)
            t0 = V.do(tensor_scalar(c8[:, 0:4], lam, -1.0, 0.0, MUL, MAX))
            t = V.do(tensor_tensor(c8[:, 0:4], c8[:, 0:4], lt[:, 0:4], ADD), t, t0)
            t = V.do(tensor_scalar(nc8[:, 0:4], c8[:, 0:4], 8.0, None, MUL), t)
            t_c8 = V.do(tensor_scalar(c8[:, 0:4], nc8[:, 0:4], -1.0, None, MUL), t)

            xp = [sb(oT + i * 516, 516) for i in range(3)]
            for x in xp:
                t_x0 = V.do(memset(x[:, 0:3], 0.0))
            xps = Ring(xp)

            def conv(dst, w0, bias, func):
                def f(o, b, tp):
                    x, xi, xf = xps.take()
                    t = S.do(activation(x[:, 3:515], PSM[:, b, 0:T2], ACT.Copy), tp, xf, t_x0)
                    w = lambda j: v2(w0 + 4 * o + j)
                    d = dst(o)
                    if bias is None:
                        ta = V.do(tensor_scalar(d, x[:, 0:512], w(0), None, MUL), t)
                    else:
                        ta = V.do(tensor_scalar(d, x[:, 0:512], w(0), v2(bias + o), MUL, ADD), t)
                    for j in range(1, 4):
                        ta = V.do(scalar_tensor_tensor(out=d, in0=x[:, j:j + 512], scalar=w(j), in1=d,
                                                                        op0=MUL, op1=ADD), ta)
                    xps.free[xi] = [ta]
                    if func is not None:
                        ta = S.do(activation(d, d, func), ta)
                    conved.append(ta)
                    return [t]
                return f

            w2 = A["w_in_2"]
            wi = [0]

            def nxt(_):
                wi[0] += 1
                return chunk(w2[wi[0] - 1])

            conved = []
            columns(2, nxt, conv(lambda o: xr[o], 88, 104, None), uX, 0, T2, t_u)
            t_xr = list(conved)

            def gelu(o, b, tp):
                return [S.do(activation(gt[o], PSM[:, b, 0:T2], ACT.Gelu_apprx_tanh), tp)]
            columns(2, nxt, gelu, uX, 0, T2, t_u)
            t_gt = S.last()

            def lru(i):
                ra, ri, aa, tt, sq = (sb(oT + 3 * 516 + n * 512, 512) for n in range(5))
                ends = []
                for n, (dst, bias) in enumerate(((ra, 108), (ri, 112))):
                    b, pi, free = pring.take()
                    tp = gemm(b, [M[:, owl + 512 * n + 128 * i:owl + 512 * n + 128 * i + 128]], [xr[i]], T2,
                              [free, t_xr[i], t_wl])
                    t = S.do(activation(dst, PSM[:, b, 0:T2], ACT.Sigmoid,
                                                                             bias=v2(bias + i)), tp, prev[0])
                    pring.free[pi] = [t]
                    ends.append(t)
                ta = S.do(activation(aa, ra, ACT.Exp, scale=c8[:, i:i + 1]), ends, t_c8)
                th = S.do(activation(tt, ra, ACT.Tanh, scale=nc8[:, i:i + 1]), ends)
                tq = S.do(activation(sq, aa, ACT.Square), ta)
                tv = V.do(scalar_tensor_tensor(out=sq, in0=sq, scalar=1.0, in1=tt, op0=ADD, op1=MUL), tq, th)
                ts = S.do(activation(sq, sq, ACT.Sqrt), tv)
                tg = G.do(tensor_tensor(ri, ri, xr[i], MUL), ends)
                tv = V.do(tensor_tensor(ri, ri, sq, MUL), tg, ts)
                tv = V.do(tensor_tensor_scan(xr[i], aa, ri, 0.0, MUL, ADD), tv)
                prev[0] = G.do(tensor_tensor(xr[i], xr[i], gt[i], MUL), tv, t_gt)

            prev = [None]
            conved = []
            dsts = q + k + v
            columns(6, nxt, conv(lambda o: dsts[o], 40, None, ACT.Silu), uX, 0, T2, t_u)
            t_qkv = list(conved)

            def silu(o, b, tp):
                return [S.do(activation(z[o], PSM[:, b, 0:T2], ACT.Silu), tp)]
            columns(2, nxt, silu, uX, 0, T2, t_u)
            t_z = S.last()
            for i in range(4):
                lru(i)
            t_lru = prev[0]
            if stage == 31:
                return

            fence()
            nsq = Ring([sb(oT + i * 512, 512) for i in range(2)])
            nrs = Ring([sb(oT + 1024 + i * 512, 512) for i in range(2)])
            ends = []
            for i, x in enumerate(q + k):
                s1, si, sf = nsq.take()
                t = S.do(activation(s1, x, ACT.Square), sf, t_qkv[i])
                b, pi, free = pring.take()
                tp = gemm(b, [con["ones"]], [s1], T2, [free, t])
                nsq.free[si] = [tp]
                r, ri, rf = nrs.take()
                S.wait(rf)
                t = finish_rstd(b, pi, T2, r, 1.0, tp)
                f = 128.0 ** -0.5 if i < 4 else 1.0
                t = V.do(scalar_tensor_tensor(out=x, in0=x, scalar=f, in1=r, op0=MUL, op1=MUL), t)
                nrs.free[ri] = [t]
                ends.append(t)
            for j in range(4):
                for src, dst in ((k, ktm), (v, vtm)):
                    b, pi, free = pring.take()
                    P.wait([free, ends, t_qkv[8:]])
                    for h in range(4):
                        tp = P.do(transpose(PSM[:, b, 128 * h:128 * h + 128],
                                                             src[h][:, 128 * j:128 * j + 128], con["ident"]))
                    t = S.do(activation(dst[j], PSM[:, b, 0:512], ACT.Copy), tp)
                    pring.free[pi] = [t]
            t_tm = S.last()
            e1 = fence()
            if stage == 32:
                return

            Ab, Xb, Nb, Kb, Eb = (Ring([sb(oT + (5 * i + n) * 512, 512) for i in range(2)]) for n in range(5))
            assert oT + 10 * 512 <= 52600, oT
            lev = lambda n: c2["lev"][:, 128 * n:128 * n + 128].unsqueeze(1).to_broadcast([128, 4, 128])
            hv = lambda ap: ap.rearrange("p (h c) -> p h c", h=4)
            hs = lambda ap, h: ap[:, 128 * h:128 * h + 128]
            bufs = [(sb(oT + 2560 * i, 512), sb(oT + 2560 * i + 512, 512), sb(oT + 2560 * i + 1024, 512),
                     sb(oT + 2560 * i + 1536, 512), sb(oT + 2560 * i + 2048, 512)) for i in range(2)]
            ident4 = con["ident"].unsqueeze(1).to_broadcast([128, 4, 128])
            ready = {}

            def prepare(j, w, freed):
                Aa, X, N1, Kb, E = bufs[w]
                for h in range(4):
                    c = 4 * j + h
                    tv = V.do(tensor_scalar(hs(E, h), c2["triu"], g[:, c:c + 1], None, MUL), freed)
                b, pi, free = pring.take()
                tp = gemm(b, [con["ones"]], [E], T2, [free, tv])
                row = hv(PSM[:, b, 0:512])
                t1 = V.do(tensor_tensor(hv(X), c2["negL"].unsqueeze(1).to_broadcast([128, 4, 128]), row, SUB), tp)
                t2 = V.do(tensor_tensor(hv(N1), c2["negU"].unsqueeze(1).to_broadcast([128, 4, 128]), row, ADD), tp)
                t3 = S.do(activation(E, PSM[:, b, 0:512], ACT.Exp), t2)
                pring.free[pi] = [t3]
                for h in range(4):
                    c = 4 * j + h
                    S.do(activation(hs(X, h), hs(X, h), ACT.Exp, bias=gc[:, c:c + 1]), t1)
                    te = S.do(activation(hs(N1, h), hs(N1, h), ACT.Exp, bias=ngc[:, c:c + 1]), t2)
                bk, pk, fk = pring.take()
                P.wait([fk])
                for h in range(4):
                    tk = P.do(matmul(PSM[:, bk, 128 * h:128 * h + 128], k[h][:, 128 * j:128 * j + 128],
                                                      k[h][:, 128 * j:128 * j + 128], start=True, stop=True,
                                                      skip_group_check=True))
                for h in range(4):
                    tq = P.do(matmul(PSM[:, bk + 1, 128 * h:128 * h + 128],
                                                      k[h][:, 128 * j:128 * j + 128], q[h][:, 128 * j:128 * j + 128],
                                                      start=True, stop=True, skip_group_check=True))
                for h in range(4):
                    c = 4 * j + h
                    ta = V.do(scalar_tensor_tensor(
                        out=hs(Aa, h), in0=PSM[:, bk, 128 * h:128 * h + 128], scalar=beta[:, c:c + 1], in1=hs(X, h),
                        op0=MUL, op1=MUL), tk, te)
                tt = V.do(tensor_tensor(atn[j], PSM[:, bk + 1, 0:512], N1, MUL), tq, te)
                pring.free[pk] = [ta, tt]
                for h in range(4):
                    tg = G.do(tensor_tensor(q[h][:, 128 * j:128 * j + 128],
                                                             q[h][:, 128 * j:128 * j + 128], hs(E, h), MUL), t3, tq)
                for h in range(4):
                    c = 4 * j + h
                    G.do(tensor_scalar(hs(Kb, h), hs(ktm[j], h), bg[:, c:c + 1], None, MUL))
                tk2 = G.last()
                for h in range(4):
                    c = 4 * j + h
                    G.do(tensor_scalar(hs(ktm[j], h), hs(ktm[j], h), dl[:, c:c + 1], None, MUL), tk2)
                    G.do(tensor_scalar(hs(vtm[j], h), hs(vtm[j], h), beta[:, c:c + 1], None, MUL))
                tx = V.do(tensor_copy(hv(X), ident4), ta)
                tx = V.do(tensor_copy(hv(XT[j]), ident4), e1)
                ready[j] = [ta, tt, tx, G.last()]
                return [ta, tx]

            def level(j, w, n, tok):
                Aa, X, N1, Kb, E = bufs[w]
                tc = G.do(tensor_tensor(hv(E), hv(Aa), lev(n), MUL), tok)
                b, pi, free = pring.take()
                P.wait([free, tc, tok])
                for h in range(4):
                    tp = P.do(matmul(PSM[:, b, 128 * h:128 * h + 128], hs(E, h), hs(XT[j], h),
                                                      start=True, stop=True, skip_group_check=True))
                tn = S.do(activation(N1, PSM[:, b, 0:512], ACT.Copy), tp)
                pring.free[pi] = [tn]
                b, pi, free = pring.take()
                P.wait([free, tn])
                for h in range(4):
                    tp2 = P.do(matmul(PSM[:, b, 128 * h:128 * h + 128], hs(X, h), hs(N1, h),
                                                       start=True, stop=True, skip_group_check=True))
                if n < 6:
                    for h in range(4):
                        tp1 = P.do(matmul(PSM[:, b + 1, 128 * h:128 * h + 128], hs(N1, h), hs(X, h),
                                                           start=True, stop=True, skip_group_check=True))
                    t1 = V.do(tensor_tensor(X, X, PSM[:, b + 1, 0:512], SUB), tp1)
                else:
                    t1 = None
                t2 = V.do(tensor_tensor(XT[j], XT[j], PSM[:, b, 0:512], SUB), tp2)
                pring.free[pi] = [t1, t2]
                return [t1, t2]

            def close(j, w, tok):
                Aa, X, N1, Kb, E = bufs[w]
                b, pi, free = pring.take()
                P.wait([free, tok, ready[j]])
                for h in range(4):
                    tp = P.do(matmul(PSM[:, b, 128 * h:128 * h + 128], hs(Kb, h), hs(XT[j], h),
                                                      start=True, stop=True, skip_group_check=True))
                t = S.do(activation(nwT[j], PSM[:, b, 0:512], ACT.Copy, scale=-1.0), tp)
                pring.free[pi] = [t]
                ready[j] = [ready[j], tok, t]
                return t

            def step(j, t_s):
                b, pi, free = pring.take()
                P.wait([free, ready[j], t_s])
                for h in range(4):
                    cs = slice(128 * h, 128 * h + 128)
                    tp = P.do(matmul(PSM[:, b, cs], XT[j][:, cs], vtm[j][:, cs], start=True,
                                                        stop=(j == 0), skip_group_check=True))
                    if j:
                        tp = P.do(matmul(PSM[:, b, cs], nwT[j][:, cs], st[:, cs], start=False,
                                                            stop=True, skip_group_check=True))
                vn = XT[j]
                tv = S.do(activation(vn, PSM[:, b, 0:512], ACT.Copy), tp)
                pring.free[pi] = [tv]
                b, pi, free = pring.take()
                P.wait([free])
                for h in range(4):
                    cs = slice(128 * h, 128 * h + 128)
                    if j:
                        P.do(matmul(PSM[:, b, cs], st[:, cs], q[h][:, 128 * j:128 * j + 128],
                                                            start=True, stop=False, skip_group_check=True))
                    to = P.do(matmul(PSM[:, b, cs], vn[:, cs], atn[j][:, cs], start=(j == 0),
                                                        stop=True, skip_group_check=True), tv)
                ts = None
                if j < 3:
                    for h in range(4):
                        cs = slice(128 * h, 128 * h + 128)
                        tp = P.do(matmul(PSM[:, b + 1, cs], ktm[j][:, cs], vn[:, cs], start=True,
                                                            stop=True, skip_group_check=True))
                    for h in range(4):
                        cs = slice(128 * h, 128 * h + 128)
                        c = 4 * j + h
                        if j == 0:
                            ts = V.do(tensor_copy(st[:, cs], PSM[:, b + 1, cs]), tp)
                        else:
                            ts = V.do(scalar_tensor_tensor(
                                out=st[:, cs], in0=st[:, cs], scalar=el[:, c:c + 1], in1=PSM[:, b + 1, cs],
                                op0=MUL, op1=ADD), tp)
                for h in range(4):
                    tq = S.do(activation(q[h][:, 128 * j:128 * j + 128],
                                                          PSM[:, b, 128 * h:128 * h + 128], ACT.Copy), to)
                pring.free[pi] = [tq, ts]
                return ts

            fr = [None, None]
            t_s = None
            for j0 in (0, 2):
                tk = [prepare(j0 + w, w, fr[w]) for w in range(2)]
                for n in range(7):
                    tk = [level(j0 + w, w, n, tk[w]) for w in range(2)]
                fr = [close(j0 + w, w, tk[w]) for w in range(2)]
                for w in range(2):
                    t_s = step(j0 + w, t_s)
            if stage == 33:
                return

            fence()
            for h in range(4):
                s1, si, sf = nsq.take()
                t = S.do(activation(s1, q[h], ACT.Square), sf)
                b, pi, free = pring.take()
                tp = gemm(b, [con["ones"]], [s1], T2, [free, t])
                nsq.free[si] = [tp]
                r, ri, rf = nrs.take()
                S.wait(rf)
                t = finish_rstd(b, pi, T2, r, 1.0 / 128, tp)
                t = V.do(scalar_tensor_tensor(out=q[h], in0=q[h], scalar=v2(120), in1=r,
                                                                    op0=MUL, op1=MUL), t)
                nrs.free[ri] = [t]
                t = G.do(tensor_tensor(q[h], q[h], z[h], MUL), t, t_z)
            columns(4, lambda c: chunk(A["w_out_2"][c]), add_in, q + xr, 0, T2, [t, t_lru])

        def cross():
            at[0] = oZ
            om, ok, ov, oq, opt = place(2048), place(2048), place(2048), place(4096), place(3072)
            osc, oty = place(1024), place(16)
            mem = [sb(om + i * 256, 256) for i in range(8)]
            K = [sb(ok + i * 256, 256) for i in range(8)]
            Vv = M[:, ov:ov + 2048].rearrange("p (j n) -> p j n", j=2)
            Q = [sb(oq + i * 512, 512) for i in range(8)]
            e0 = fence()
            s_m = newsem("s_m")
            t_m = load(Y, s_m, sb(om, 2048), A["mem"], e0)
            sqs = Ring([sb(oNs + i * 512, 512) for i in range(3)])
            rs = sb(oNs + 1536, 512)
            t = rms_rstd(mem, 256, rs, sqs, 1.0 / D, t_m)
            t_mu = scaled(mem, mem, lambda k: v2(16 + k), rs, 256, t)
            t_u = norm_in(8, fence())

            def kcopy(o, b, tp):
                return [S.do(activation(K[o], PSM[:, b, 0:256], ACT.Copy), tp)]
            columns(4, lambda c: chunk(A["xattn_wkv_2"][c]), kcopy, mem, 0, 256, t_mu)
            for c in range(4):
                b0, wslot, tw = chunk(A["xattn_wkv_2"][4 + c])
                w = b0.rearrange("p (k n) -> p k n", k=8)
                for j in range(2):
                    b, pi, free = pring.take()
                    tp = gemm(b, [m[:, 128 * j:128 * j + 128] for m in mem], [w[:, k, :] for k in range(8)], 256,
                              [free, tw, t_mu])
                    t = V.do(tensor_copy(Vv[:, j, 256 * c:256 * c + 256], PSM[:, b, 0:256]), tp)
                    pring.free[pi] = [t]
                wring.free[wslot] = [tp]

            def qcopy(o, b, tp):
                return [S.do(activation(Q[o], PSM[:, b, 0:T2], ACT.Copy, scale=0.0625), tp)]
            columns(4, lambda c: chunk(A["xattn_wq_2"][c]), qcopy, uX, 0, T2, t_u)
            t_qkv = [S.last(), V.last()]
            scr = Ring([sb(osc + i * 256, 256) for i in range(4)])
            tiny = Ring([sb(oty + i * 4, 4) for i in range(4)])
            ptr = Ring([sb(opt + i * 1024, 1024) for i in range(3)])
            hold = Ring([pring.bufs.pop(), pring.bufs.pop()])
            hold.free = [pring.free.pop(), pring.free.pop()]
            pring.i = -1
            av = {}
            hb = {}

            def scores(u):
                h, n = divmod(u, 4)
                b, pi, free = pring.take()
                tp = gemm(b, [Q[2 * h + i][:, 128 * n:128 * n + 128] for i in range(2)], [K[2 * h + i] for i in range(2)],
                          256, [free, t_qkv])
                y, yi, yf = tiny.take()
                s, si, sf = scr.take()
                t = V.do(tensor_reduce(y[:, 0:1], PSM[:, b, 0:256], AX.X, MAX, negate=True), tp, yf)
                te = S.do(activation(s, PSM[:, b, 0:256], ACT.Exp, bias=y[:, 0:1], accum_out=y[:, 1:2]), t, sf)
                pring.free[pi] = [te]
                t = V.do(reciprocal(y[:, 2:3], y[:, 1:2]), te)
                t = V.do(tensor_scalar(s, s, y[:, 2:3], None, MUL), t)
                tiny.free[yi] = [t]
                av[u] = (s, si, t)

            def turn(u):
                h, n = divmod(u, 4)
                s, si, t = av[u]
                if n == 0:
                    b, pi, free = hold.take()
                    hb[h] = (b, pi)
                    P.wait([free])
                b, pi = hb[h]
                for m in range(2):
                    tp = P.do(transpose(PSM[:, b + m, 128 * n:128 * n + 128],
                                                         s[:, 128 * m:128 * m + 128], con["ident"]), t)
                scr.free[si] = [tp]
                if n == 3:
                    p, ti, tf = ptr.take()
                    t = S.do(activation(p.rearrange("p (m q) -> p m q", m=2), PSM[:, b:b + 2, :], ACT.Copy),
                             tp, tf)
                    hold.free[pi] = [t]
                    hb[h] = (p, ti, t)

            def outs(h):
                p, ti, t = hb[h]
                for i in range(2):
                    b, pi, free = pring.take()
                    tp = gemm(b, [Vv[:, m, 256 * h + 128 * i:256 * h + 128 * i + 128] for m in range(2)],
                              [p[:, 512 * m:512 * m + 512] for m in range(2)], T2, [free, t])
                    tv = V.do(tensor_copy(Q[2 * h + i], PSM[:, b, 0:T2]), tp)
                    pring.free[pi] = [tv]
                ptr.free[ti] = [tp]

            for u in range(16 + 4):
                if u < 16:
                    scores(u)
                if 2 <= u < 18:
                    turn(u - 2)
                if u >= 6 and (u - 6) % 4 == 0:
                    outs((u - 6) // 4)
            outs(3)
            for _ in range(2):
                pring.bufs.append(hold.bufs.pop())
                pring.free.append(hold.free.pop())
            columns(4, lambda c: chunk(A["xattn_wo_2"][c]), add_in, Q, 0, T2, [V.last()])

        def peer():
            at[0] = oZ
            oE1, oE2, oGt = place(512), place(512), place(512)
            oY = at[0]
            oQ = place(8192)
            e0 = fence()
            t_u = norm_in(24, e0)
            Q = [sb(oQ + i * 512, 512) for i in range(16)]
            oKeys = place(2048)
            s_k = newsem("s_keys")
            t_k = load(Y, s_k, sb(oKeys, 2048), A["subkeys"], e0)

            def qcopy(o, b, tp):
                return [S.do(activation(Q[o], PSM[:, b, 0:T2], ACT.Copy), tp)]
            columns(8, lambda c: chunk(A["peer_wq_2"][c]), qcopy, uX, 0, T2, t_u)
            t_q = S.last()
            scs = Ring([sb(place(2048), 2048) for _ in range(2)])
            oCd, oEq = place(2048), place(2048)
            cand, eq = sb(oCd, 2048), sb(oEq, 2048)
            tv, tif, bv, gv, af, bf, e1, e2 = (sb(place(n), n) for n in (256, 256, 128, 128, 128, 128, 128, 128))
            sm = sb(place(16), 16)
            ti = sb(place(256), 256).bitcast(U32)
            bp = sb(place(128), 128).bitcast(U32)
            ap_, bp_ = sb(place(128), 128).bitcast(U32), sb(place(128), 128).bitcast(U32)
            assert at[0] <= oNs
            LOW = -3.0e38
            fence()
            te = None
            for n in range(4):
                sc, si, sf = scs.take()
                for c in range(4):
                    b, pi, free = pring.take()
                    P.wait([free, t_q, t_k])
                    for i in range(4):
                        hp = 4 * c + i
                        tp = P.do(matmul(
                            PSM[:, b, 128 * i:128 * i + 128], Q[hp][:, 128 * n:128 * n + 128],
                            M[:, oKeys + 128 * hp:oKeys + 128 * hp + 128], start=True, stop=True, skip_group_check=True))
                    t = S.do(activation(sc[:, 512 * c:512 * c + 512], PSM[:, b, 0:512], ACT.Copy),
                             tp, sf)
                    pring.free[pi] = [t]
                t_sc = t

                def top16(vals, size, count, mx, ix, tok):
                    part = lambda i: vals[:, size * i:size * i + size]
                    for half in range(2):
                        o = 8 * half
                        for i in range(count):
                            t = V.do(max8(mx[:, 16 * i + o:16 * i + o + 8], part(i)), tok)
                        tok = t
                        for i in range(count):
                            t = V.do(max_index(ix[:, 16 * i + o:16 * i + o + 8],
                                                                mx[:, 16 * i + o:16 * i + o + 8], part(i)), tok)
                        tok = t
                        if half == 0:
                            for i in range(count):
                                t = V.do(match_replace(part(i), mx[:, 16 * i:16 * i + 8], part(i), LOW),
                                         tok)
                            tok = t
                    return tok

                t = top16(sc, 128, 16, tv, ti, [t_sc, te])
                scs.free[si] = [t]
                V.do(tensor_copy(tif, ti), t)
                tvv = tv.rearrange("p (h two k) -> p h two k", h=8, two=2)
                c4 = cand.rearrange("p (h i j) -> p h i j", h=8, i=16)
                for h in range(8):
                    t = V.do(tensor_tensor(
                        c4[:, h], tvv[:, h, 0, :].unsqueeze(2).to_broadcast([128, 16, 16]),
                        tvv[:, h, 1, :].unsqueeze(1).to_broadcast([128, 16, 16]), ADD), t)
                t = top16(cand, 256, 8, bv, bp, t)
                b3 = lambda ap: ap.rearrange("p (h k) -> p h k", h=8)
                t1 = V.do(tensor_tensor(b3(gv), b3(bv), b3(bv)[:, :, 0:1].to_broadcast([128, 8, 16]), SUB), t)
                t1 = S.do(activation(gv, gv, ACT.Exp), t1)
                t2 = V.do(tensor_scalar(ap_, bp, 4, None, ALU.logical_shift_right), t)
                t3 = V.do(tensor_scalar(bp_, bp, 15, None, ALU.bitwise_and), t)
                t2 = V.do(tensor_copy(af, ap_), t2)
                t3 = V.do(tensor_copy(bf, bp_), t3)
                iota = c2["iota"]
                q3 = eq.rearrange("p (k j) -> p k j", j=16)
                q4 = eq.rearrange("p (h k j) -> p h k j", h=8, k=16)
                i4 = tif.rearrange("p (h two j) -> p h two j", h=8, two=2)
                for s_, (pos, dst) in enumerate(((af, e1), (bf, e2))):
                    t = V.do(tensor_tensor(
                        q3, pos.unsqueeze(2).to_broadcast([128, 128, 16]),
                        iota[:, 0:16].unsqueeze(1).to_broadcast([128, 128, 16]), ALU.is_equal), t2, t3, t)
                    for h in range(8):
                        tt = V.do(tensor_tensor(
                            q4[:, h], q4[:, h], i4[:, h, s_, :].unsqueeze(1).to_broadcast([128, 16, 16]), MUL), t)
                    t = V.do(tensor_reduce(dst, q3, AX.X, ADD), tt, te)
                t1 = V.do(tensor_reduce(sm[:, 0:8], b3(gv), AX.X, ADD), t1)
                t1 = V.do(reciprocal(sm[:, 8:16], sm[:, 0:8]), t1)
                t1 = V.do(tensor_tensor(b3(gv), b3(gv), sm[:, 8:16].unsqueeze(2).to_broadcast([128, 8, 16]),
                                                    MUL), t1)
                b, pi, free = pring.take()
                P.wait([free, t, t1])
                for i, x in enumerate((e1, e2, gv)):
                    tp = P.do(transpose(PSM[:, b, 128 * i:128 * i + 128], x, con["ident"]))
                dst = M[:, oE1:oE1 + 1536].rearrange("p (i t) -> p i t", i=3)[:, :, 128 * n:128 * n + 128]
                te = S.do(activation(
                    dst, PSM[:, b, 0:384].rearrange("p (i t) -> p i t", i=3), ACT.Copy), tp)
                pring.free[pi] = [te]
            if stage == 35:
                t = V.do(tensor_copy(xT[0], sb(oE1, 512)), te)
                t = V.do(tensor_copy(xT[1], sb(oE2, 512)), te)
                t = V.do(tensor_copy(xT[2], sb(oGt, 512)), te)
                return

            fence()
            at[0] = oY
            oG_, oA_ = place(512 * 32), place(8 * 512)
            onA = Ring([sb(place(512), 512) for _ in range(3)])
            onB = Ring([sb(place(128), 128) for _ in range(3)])
            acts = Ring([sb(oA_ + i * 512, 512) for i in range(8)])
            E1, E2, Gt = sb(oE1, 512), sb(oE2, 512), sb(oGt, 512)
            Gv = M[:, oG_:oG_ + 16384].rearrange("p (t n) -> p t n", n=32)
            t_g_free = None
            iota = c2["iota"]
            for qd in range(4):
                for t32 in range(16):
                    b, pi, free = pring.take()
                    P.wait([free])
                    for t4 in range(8):
                        a, ai, af_ = onA.take()
                        o, oi, of = onB.take()
                        for i in range(4):
                            t = 32 * t32 + 4 * t4 + i
                            ta = V.do(tensor_scalar(
                                a[:, 128 * i:128 * i + 128], iota, E1[:, t:t + 1], Gt[:, t:t + 1],
                                ALU.is_equal, MUL), af_)
                            tb = G.do(tensor_scalar(
                                o[:, 32 * i:32 * i + 32], iota[:, 32 * qd:32 * qd + 32], E2[:, t:t + 1], None,
                                ALU.is_equal), of)
                        P.wait([ta, tb])
                        for i in range(4):
                            c = 4 * t4 + i
                            tp = P.do(matmul(
                                PSM[:, b + c // 16, 32 * (c % 16):32 * (c % 16) + 32], a[:, 128 * i:128 * i + 128],
                                o[:, 32 * i:32 * i + 32], start=True, stop=True, skip_group_check=True))
                        onA.free[ai] = [tp]
                        onB.free[oi] = [tp]
                    t_g = S.do(activation(
                        M[:, oG_ + 1024 * t32:oG_ + 1024 * t32 + 1024].rearrange("p (a n) -> p a n", a=2),
                        PSM[:, b:b + 2, :], ACT.Copy), tp, t_g_free)
                    pring.free[pi] = [t_g]
                for gr in range(4):
                    res = []
                    for c in range(4):
                        ci = 16 * qd + 4 * gr + c
                        ub, us, tu = chunk(A["peer_u"][ci])
                        w = ub.rearrange("p (k n) -> p k n", k=8)
                        for i in range(2):
                            b, pi, free = pring.take()
                            tp = gemm(b, [w[:, k, 128 * i:128 * i + 128] for k in range(8)], uX, T2, [free, tu])
                            a, ai, af_ = acts.take()
                            t = S.do(activation(a, PSM[:, b, 0:T2], ACT.Gelu_apprx_tanh), tp, af_)
                            pring.free[pi] = [t]
                            el_ = 8 * gr + 2 * c + i
                            t = V.do(tensor_tensor(a, a, Gv[:, :, el_], MUL), t, t_g)
                            res.append((a, ai, t))
                        wring.free[us] = [tp]
                    t_g_free = res[-1][2]
                    vs = [chunk(A["peer_v"][16 * qd + 4 * gr + c]) for c in range(4)]
                    for d in range(8):
                        b, pi, free = pring.take()
                        tp = gemm(b, [vs[i // 2][0][:, 1024 * (i % 2) + 128 * d:1024 * (i % 2) + 128 * d + 128]
                                      for i in range(8)], [r[0] for r in res], T2,
                                  [free, [x[2] for x in vs], [r[2] for r in res]])
                        pring.free[pi] = add_in(d, b, tp)
                    for x in vs:
                        wring.free[x[1]] = [tp]
                    for r in res:
                        acts.free[r[1]] = [tp]

        def second():
            for name, f in ((34, mixer), (36, cross), (38, peer)):
                f()
                if stage and stage <= name:
                    return
            norm_in(32, fence())

        t_lg0 = [None]
        layer(0, t_h)
        if stage >= 20 or stage == 0:
            layer(1, now())

        if stage == 0 or stage >= 30:
            second()

        s_out = newsem("s_out")
        if stage and stage < 30:
            t_out = load(Y, s_out, out.rearrange("(k p) t -> p k t", p=128),
                         M[:, oH:oH + 8 * TT].rearrange("p (k t) -> p k t", k=8), now())
        else:
            src = oH + 16 if stage else oU + 16
            t_out = load(Y, s_out, out.rearrange("(k p) t -> p k t", p=128),
                         M[:, src - 16:src - 16 + 8 * TT].rearrange("p (k t) -> p k t", k=8)[:, :, 16:], now())
        Y.wait([t_out])

        block = ctx.enter_context(nc.Block())

        def emit(q):
            def f(e):
                for op in q.ops:
                    op(e)
            return f

        block.sync(emit(Y))
        block.tensor(emit(P))
        block.vector(emit(V))
        block.scalar(emit(S))
        block.gpsimd(emit(G))


def chunks(w, kt, cols):
    K, Nn = w.shape
    return w.reshape(K // (128 * kt), kt, 128, Nn // cols, cols).transpose(3, 0, 2, 1, 4).reshape(-1, 128, kt * cols)


def constants():
    import numpy as np
    f = np.float32
    c = np.zeros((128, C_W), f)

    def put(n, a):
        o, w = C_OFF[n]
        c[:a.shape[0], o:o + a.shape[1]] = a

    p = np.arange(128)
    put("ident", np.eye(128, dtype=f))
    put("ones", np.ones((128, 128), f))
    put("onesm", np.full((128, 128), 1 / 128, f))
    for name, half, theta, rot in (("R", 32, 10000.0, 64), ("A", 8, 500000.0, 16)):
        perm = np.zeros((128, 128), f)
        cos = np.ones((128, TT), f)
        sin = np.zeros((128, TT), f)
        freqs = np.power(f(theta), -np.arange(0, rot, 2, dtype=f) / f(rot)).astype(f)
        ang = np.arange(TT).astype(f)[None, :] * freqs[:, None]
        for m in range(128):
            d = m % 64
            if d < half:
                perm[m + half, m] = -1
            elif d < rot:
                perm[m - half, m] = 1
            if d < rot:
                cos[m] = np.cos(ang[d % half])
                sin[m] = np.sin(ang[d % half])
        put("perm" + name, perm)
        put("cos" + name, cos)
        put("sin" + name, sin)
    put("rel", (np.arange(928)[None, :] - 400 - p[:, None]).astype(f))
    band = np.zeros((128, 384), f)
    k = p[None, :]
    band[:, 0:128][k < p[:, None]] = -1e30
    band[:, 256:384][k > p[:, None]] = -1e30
    z = np.zeros((128, 16), f)
    put("mA", np.concatenate([z, band], 1))
    put("mB", np.concatenate([z, band[:, 128:]], 1))
    mc = np.zeros((16, 144), f)
    mc[:, 16:][np.arange(128)[None, :] > 112 + np.arange(16)[:, None]] = -1e30
    put("mC", mc)
    put("eps", np.full((128, 1), 1e-6, f))
    return c


def constants2():
    import numpy as np
    c = np.zeros((128, C2_W), np.float32)
    i, j = np.arange(128)[:, None], np.arange(128)[None, :]

    def put(n, a, at=0):
        o, w = C2_OFF[n]
        c[:, o + at:o + at + a.shape[1]] = a

    put("triu", (i <= j).astype(np.float32))
    put("negL", np.where(j < i, 0, -1e30))
    put("negU", np.where(j >= i, 0, -1e30))
    for n in range(7):
        h = 1 << n
        put("lev", ((i // (2 * h) == j // (2 * h)) & (i // h % 2 == 1) & (j // h % 2 == 0)).astype(np.float32), 128 * n)
    put("iota", np.broadcast_to(j, (128, 128)))
    return c


STAGE = 0


def kernel(**inputs):
    import numpy as np
    import concourse.bacc as _bacc
    from concourse import mybir as _mybir
    from concourse.bass_utils import run_bass_kernel_spmd as _run

    I = {k: np.asarray(v) for k, v in inputs.items()}
    f = np.float32
    stage = STAGE
    arr = {"consts": constants()}

    def cols(v):
        return v.reshape(-1, 128).T

    def rep(v):
        return np.broadcast_to(v.reshape(1, -1), (128, v.size))

    norms = [I[n][l] for l in range(2) for n in ("norm_mix_pre", "norm_mix_post", "norm_ff_pre", "norm_ff_post")]
    arr["vec1"] = np.concatenate([cols(v) for v in norms] + [rep(I["attn_sink"]), rep(I["ret_decay"])], 1)
    h = np.concatenate([I["meta_tokens"], I["x"][0]], 0).T
    arr["hin"] = h.reshape(8, 128, TT).transpose(1, 0, 2).reshape(128, 8 * TT)
    w = I["w_in"]
    q0, q1, v0, g0, a0, k0, va0, r0, s0 = np.cumsum([0, 512, 512, 1024, 1024, 512, 128, 128, 1024])
    pair = np.concatenate([np.arange(64) + 64 * x for a in range(4) for x in (a, a + 4)])
    order = np.concatenate([np.arange(q0, v0), a0 + pair, np.arange(k0, r0), np.arange(v0, a0), np.arange(r0, 5888)])
    arr["w_in"] = np.stack([chunks(w[l][:, order], 8, 256) for l in range(2)])
    arr["w_ret_o"] = np.stack([chunks(I["w_ret_o"][l], 8, 256) for l in range(2)])
    arr["w_att_o"] = np.stack([chunks(I["w_att_o"][l][pair], 4, 512) for l in range(2)])
    arr["w_mix_o"] = np.stack([chunks(I["w_mix_o"][l], 8, 256) for l in range(2)])
    arr["w_ff1"] = np.stack([chunks(I["w_ff1"][l], 8, 256) for l in range(2)])
    arr["w_ff2"] = np.stack([chunks(I["w_ff2"][l], 16, 128) for l in range(2)])

    arr["consts2"] = constants2()
    conv = I["conv_qkv_w_2"][0].reshape(4, 12, 128).transpose(2, 1, 0).reshape(128, 48)
    lconv = I["lru_conv_w_2"][0].reshape(4, 4, 128).transpose(2, 1, 0).reshape(128, 16)
    vec2 = [cols(I[n][0]) for n in ("norm_mix_w_2", "norm_xattn_w_2", "norm_mem_w_2", "norm_ffn_w_2")]
    vec2 += [cols(I["norm_final_w_2"]), conv, lconv]
    vec2 += [cols(I[n][0]) for n in ("lru_conv_b_2", "lru_ba_2", "lru_bx_2", "lru_lambda_2", "gdn_norm_w_2")]
    vec2 += [rep(I["gdn_a_log_2"]), rep(I["gdn_dt_bias_2"])]
    arr["vec2"] = np.concatenate(vec2, 1)
    w = I["w_in_2"][0]
    order = np.concatenate([np.arange(2056, 3080), np.arange(0, 2048)])
    arr["w_in_2"] = chunks(w[:, order], 8, 256)
    arr["w_ab"] = w[:, 2048:2056].reshape(8, 128, 8).transpose(1, 0, 2).reshape(128, 64)
    lru = np.zeros((128, 2, 4, 128), f)
    for n, name in enumerate(("lru_wa_2", "lru_wx_2")):
        for g in range(8):
            o = 64 * (g % 2)
            lru[o:o + 64, n, g // 2, o:o + 64] = I[name][0, g]
    arr["w_lru"] = lru.reshape(128, 1024)
    arr["w_out_2"] = chunks(I["w_out_2"][0], 8, 256)
    arr["mem"] = I["mem_2"][0].T.reshape(8, 128, 256).transpose(1, 0, 2).reshape(128, 2048)
    for n in ("xattn_wq_2", "xattn_wkv_2", "xattn_wo_2", "peer_wq_2"):
        arr[n] = chunks(I[n][0], 8, 256)
    arr["subkeys"] = I["peer_subkeys_2"][0].reshape(16, 128, 128).transpose(2, 0, 1).reshape(128, 2048)
    u = I["peer_u_2"][0].reshape(128, 64, 2, 8, 128)
    arr["peer_u"] = u.transpose(1, 4, 3, 2, 0).reshape(64, 128, SL)
    arr["peer_v"] = I["peer_v_2"][0].reshape(128, 64, 2048).transpose(1, 0, 2)

    nc = _bacc.Bacc("TRN2", target_bir_lowering=False, num_devices=1)
    arrays, A = {}, {}
    for n, a in arr.items():
        a = np.ascontiguousarray(a)
        arrays[n + "_dram"] = a
        A[n] = nc.dram_tensor(n + "_dram", a.shape, _mybir.dt.from_np(a.dtype), kind="ExternalInput").ap()
    shape = (1024, 528) if 0 < stage < 30 else (1024, 512)
    out = nc.dram_tensor("out_dram", shape, _mybir.dt.float32, kind="ExternalOutput").ap()
    program(nc, A, out, stage)
    r = _run(nc, [arrays], core_ids=[0])
    got = r.results[0]["out_dram"]
    return np.ascontiguousarray(got.T).reshape(1, shape[1], 1024)
```
